# Optimizing a Trainium2 kernel written in Bass

```python
import math, functools
import jax
import jax.numpy as jnp
from jax import lax
import numpy as np

D_MODEL = 1024
BATCH = 1
SEQ = 256
DEPTH = 2

GRID_W = 64
CTX_LEN = 256
N_MIXERS = 3
NORM_EPS = 1e-6
CHUNK = 64

GLA_HEADS = 4
GLA_KEY = D_MODEL // 2
GLA_VAL = D_MODEL
GLA_DK = GLA_KEY // GLA_HEADS
GLA_DV = GLA_VAL // GLA_HEADS
GLA_RANK = 16
GLA_GATE_NORM = 16.0
GLA_IN = 2 * GLA_KEY + 2 * GLA_VAL + 2 * GLA_RANK

RW_HEAD = 64
RW_HEADS = D_MODEL // RW_HEAD
RW_DECAY_LORA = 64
RW_A_LORA = 64
RW_G_LORA = 160
RW_GN_EPS = 64e-5

MB_INNER = 2 * D_MODEL
MB_HEADDIM = 64
MB_HEADS = MB_INNER // MB_HEADDIM
MB_GROUPS = 4
MB_HPG = MB_HEADS // MB_GROUPS
MB_STATE = 128
MB_BC = MB_GROUPS * MB_STATE
MB_CONV_W = 5
MB_CONV_CH = MB_INNER + 2 * MB_BC
MB_IN = 2 * MB_INNER + 2 * MB_BC + 2 * MB_HEADS

D_FF = 2816
N_EXPERTS = 8
TOP_K = 2
D_FF_EXPERT = 3584

N_GLA = len(range(0, DEPTH, N_MIXERS))
N_RWKV = len(range(1, DEPTH, N_MIXERS))
N_MAMBA = len(range(2, DEPTH, N_MIXERS))
N_DENSE = len(range(0, DEPTH, 2))
N_MOE = len(range(1, DEPTH, 2))

kernel_name = 'hybrid_gla_rwkv7_ssd_moe_prefix_dit'

def rmsnorm(x, g):
    xf = x.astype(jnp.float32)
    y = xf * lax.rsqrt(jnp.mean(xf * xf, axis=-1, keepdims=True) + NORM_EPS)
    return (y * g.astype(jnp.float32)).astype(x.dtype)

def modulate(x, gain, shift, scale):
    return rmsnorm(x, gain) * (1 + scale) + shift

def swiglu(h, w_gu, w_d):
    a, b = jnp.split(h @ w_gu, 2, axis=-1)
    return (jax.nn.silu(a) * b) @ w_d

def moe_ffn(h, router, w_gu, w_d):
    logits = (h @ router).astype(jnp.float32)
    top_logits, top_idx = lax.top_k(logits, TOP_K)
    weights = jax.nn.softmax(top_logits, axis=-1)
    combine = jnp.sum(jax.nn.one_hot(top_idx, N_EXPERTS, dtype=jnp.float32) * weights[..., None], axis=-2)
    out = jnp.zeros(h.shape, jnp.float32)
    for e in range(N_EXPERTS):
        out = out + combine[..., e:e + 1] * swiglu(h, w_gu[e], w_d[e])
    return out.astype(h.dtype)

def quad_shift(x, rows):
    bsz, n, d = x.shape
    q = d // 4
    g = x.reshape(bsz, rows, GRID_W, d)
    left = jnp.pad(g[:, :, :-1, :q], ((0, 0), (0, 0), (1, 0), (0, 0)))
    right = jnp.pad(g[:, :, 1:, q:2 * q], ((0, 0), (0, 0), (0, 1), (0, 0)))
    up = jnp.pad(g[:, :-1, :, 2 * q:3 * q], ((0, 0), (1, 0), (0, 0), (0, 0)))
    down = jnp.pad(g[:, 1:, :, 3 * q:], ((0, 0), (0, 1), (0, 0), (0, 0)))
    return jnp.concatenate([left, right, up, down], axis=-1).reshape(bsz, n, d)

def seq_shift(x):
    h = x.shape[-1] // 2
    prev = jnp.pad(x[:, :-1, :h], ((0, 0), (1, 0), (0, 0)))
    nxt = jnp.pad(x[:, 1:, h:], ((0, 0), (0, 1), (0, 0)))
    return jnp.concatenate([prev, nxt], axis=-1)

def centred_dwconv(x, w, b):
    pad = w.shape[0] // 2
    out = lax.conv_general_dilated(x, w[:, None, :].astype(x.dtype), window_strides=(1,),
                                   padding=[(pad, pad)], dimension_numbers=('NWC', 'WIO', 'NWC'),
                                   feature_group_count=x.shape[-1])
    return out + b

def two_pass(scan_fn, ctx_in, lat_in, s0, reverse):
    flip = (lambda t: jnp.flip(t, axis=1)) if reverse else (lambda t: t)
    y_ctx, s_ctx = scan_fn(*(flip(t) for t in ctx_in), s0)
    y_lat, _ = scan_fn(*(flip(t) for t in lat_in), s_ctx)
    return flip(y_ctx), flip(y_lat)

def gla_chunk_scan(q, k, v, log_a, s0):
    bsz, length, h, _ = q.shape
    n = length // CHUNK

    def chunks(t):
        return jnp.moveaxis(t.reshape(bsz, n, CHUNK, h, t.shape[-1]), 1, 0)

    mask = jnp.tril(jnp.ones((CHUNK, CHUNK), dtype=bool))

    def step(s, inp):
        qc, kc, vc, lac = inp
        b = jnp.cumsum(lac, axis=1)
        b_last = b[:, -1:]
        q_dec = qc * jnp.exp(b)
        att = jnp.einsum('bthk,bshk->bhts', q_dec, kc * jnp.exp(-b))
        att = jnp.where(mask, att, 0.0)
        y = jnp.einsum('bhts,bshv->bthv', att, vc) + jnp.einsum('bthk,bhkv->bthv', q_dec, s)
        s = s * jnp.exp(b_last[:, 0])[..., None] + jnp.einsum('bshk,bshv->bhkv', kc * jnp.exp(b_last - b), vc)
        return s, y

    s, y = lax.scan(step, s0, (chunks(q), chunks(k), chunks(v), chunks(log_a)))
    return jnp.moveaxis(y, 0, 1).reshape(bsz, length, h, v.shape[-1]), s

def ssd_chunk_scan(xdt, log_a, bm, cm, s0):
    bsz, length = xdt.shape[:2]
    n = length // CHUNK

    def chunks(t):
        return jnp.moveaxis(t.reshape((bsz, n, CHUNK) + t.shape[2:]), 1, 0)

    mask = jnp.tril(jnp.ones((CHUNK, CHUNK), dtype=bool))[None, :, :, None, None]

    def step(s, inp):
        xc, lac, bc, cc = inp
        cum = jnp.cumsum(lac, axis=1)
        seg = cum[:, :, None] - cum[:, None, :]
        decay = jnp.exp(jnp.where(mask, seg, -jnp.inf))
        cb = jnp.einsum('btgn,bsgn->btsg', cc, bc)
        y = jnp.einsum('btsg,btsgh,bsghp->btghp', cb, decay, xc)
        y = y + jnp.einsum('btgn,bghpn->btghp', cc, s) * jnp.exp(cum)[..., None]
        cum_last = cum[:, -1]
        s = s * jnp.exp(cum_last)[..., None, None] + jnp.einsum(
            'bsgn,bsghp->bghpn', bc, xc * jnp.exp(cum_last[:, None] - cum)[..., None])
        return s, y

    s, y = lax.scan(step, s0, (chunks(xdt), chunks(log_a), chunks(bm), chunks(cm)))
    return jnp.moveaxis(y, 0, 1).reshape(xdt.shape), s

def rwkv_scan(r, decay, k, v, kk, a, s0):
    def step(s, inp):
        rt, wt, kt, vt, kkt, at = inp
        sa = jnp.einsum('bhvk,bhk->bhv', s, -kkt)
        s = s * wt[:, :, None, :] + sa[..., None] * (kkt * at)[:, :, None, :] + vt[..., None] * kt[:, :, None, :]
        return s, jnp.einsum('bhvk,bhk->bhv', s, rt)

    s, y = lax.scan(step, s0, tuple(jnp.moveaxis(t, 1, 0) for t in (r, decay, k, v, kk, a)))
    return jnp.moveaxis(y, 0, 1), s

def gla_mixer(hc, hl, w_in, w_g2, b_g, norm_g, w_out, need_ctx):
    f32 = jnp.float32
    splits = [GLA_KEY, 2 * GLA_KEY, 2 * GLA_KEY + GLA_VAL, 2 * GLA_KEY + 2 * GLA_VAL,
              2 * GLA_KEY + 2 * GLA_VAL + GLA_RANK]

    def heads(t, d):
        return t.astype(f32).reshape(t.shape[:-1] + (GLA_HEADS, d))

    def project(h):
        q, k, v, r, g_f, g_b = jnp.split(h @ w_in, splits, axis=-1)
        log_a = [heads(jax.nn.log_sigmoid((g @ w_g2[d] + b_g[d]).astype(f32)) / GLA_GATE_NORM, GLA_DK)
                 for d, g in enumerate((g_f, g_b))]
        return heads(q, GLA_DK) * GLA_DK ** -0.5, heads(k, GLA_DK), heads(v, GLA_DV), r, log_a

    qc, kc, vc, rc, lac = project(hc)
    ql, kl, vl, rl, lal = project(hl)
    s0 = jnp.zeros((hl.shape[0], GLA_HEADS, GLA_DK, GLA_DV), f32)
    yc_f, yl_f = two_pass(gla_chunk_scan, (qc, kc, vc, lac[0]), (ql, kl, vl, lal[0]), s0, False)
    yc_b, yl_b = two_pass(gla_chunk_scan, (qc, kc, vc, lac[1]), (ql, kl, vl, lal[1]), s0, True)

    def finish(y, r):
        yn = y * lax.rsqrt(jnp.mean(y * y, axis=-1, keepdims=True) + NORM_EPS) * norm_g
        yn = yn.reshape(y.shape[:2] + (GLA_VAL,)).astype(r.dtype)
        return (yn * jax.nn.silu(r)) @ w_out

    y_ctx = finish(yc_f + yc_b, rc) if need_ctx else None
    return y_ctx, finish(yl_f + yl_b, rl)

def rwkv_mixer(hc, hl, rows, mu, w_rkv, w_o, w0, w1, w2, a0, a1, a2, g1, g2, k_k, k_a, r_k,
               ln_g, ln_b, need_ctx):
    f32 = jnp.float32

    def heads(t):
        return t.astype(f32).reshape(t.shape[:-1] + (RW_HEADS, RW_HEAD))

    def project(h, shifted):
        xx = shifted - h
        xr, xw, xk, xv, xa, xg = (h + xx * mu[j] for j in range(6))
        r, k, v = xr @ w_rkv[0], xk @ w_rkv[1], xv @ w_rkv[2]
        g = jax.nn.sigmoid(xg @ g1) @ g2
        kk = heads(k * k_k)
        kk = kk / jnp.maximum(jnp.linalg.norm(kk, axis=-1, keepdims=True), 1e-12)
        per_dir = []
        for d in range(2):
            w = -jax.nn.softplus(-(w0[d] + jnp.tanh(xw @ w1[d]) @ w2[d]).astype(f32)) - 0.5
            a = jax.nn.sigmoid(a0[d] + (xa @ a1[d]) @ a2[d])
            kd = k * (1.0 + (a - 1.0) * k_a)
            per_dir.append((jnp.exp(-jnp.exp(heads(w))), heads(kd), heads(a)))
        return heads(r), heads(v), kk, g, per_dir

    rc, vc, kkc, gc, dc = project(hc, seq_shift(hc))
    rl, vl, kkl, gl, dl = project(hl, quad_shift(hl, rows))
    s0 = jnp.zeros((hl.shape[0], RW_HEADS, RW_HEAD, RW_HEAD), f32)
    ys = []
    for d in range(2):
        ys.append(two_pass(rwkv_scan, (rc, dc[d][0], dc[d][1], vc, kkc, dc[d][2]),
                           (rl, dl[d][0], dl[d][1], vl, kkl, dl[d][2]), s0, d == 1))

    def finish(y, r, v, dirs, g):
        bsz, length = y.shape[:2]
        mean = jnp.mean(y, axis=-1, keepdims=True)
        var = jnp.mean(jnp.square(y - mean), axis=-1, keepdims=True)
        yn = ((y - mean) * lax.rsqrt(var + RW_GN_EPS)).reshape(bsz, length, D_MODEL) * ln_g + ln_b
        bonus = (jnp.sum(r * dirs[0][1] * r_k, axis=-1, keepdims=True)
                 + jnp.sum(r * dirs[1][1] * r_k, axis=-1, keepdims=True)) * v
        out = yn + bonus.reshape(bsz, length, D_MODEL)
        return (out.astype(g.dtype) * g) @ w_o

    y_ctx = finish(ys[0][0] + ys[1][0], rc, vc, dc, gc) if need_ctx else None
    return y_ctx, finish(ys[0][1] + ys[1][1], rl, vl, dl, gl)

def mamba_mixer(hc, hl, w_in, conv_w, conv_b, dt_bias, a_log, d_skip, norm_g, w_out, need_ctx):
    f32 = jnp.float32
    splits = [MB_INNER, MB_INNER + MB_CONV_CH, MB_INNER + MB_CONV_CH + MB_HEADS]

    def project(h):
        bsz, length, _ = h.shape
        z, xbc, dt_f, dt_b = jnp.split(h @ w_in, splits, axis=-1)
        xbc = jax.nn.silu(centred_dwconv(xbc, conv_w, conv_b)).astype(f32)
        xs, bm, cm = jnp.split(xbc, [MB_INNER, MB_INNER + MB_BC], axis=-1)
        xs = xs.reshape(bsz, length, MB_GROUPS, MB_HPG, MB_HEADDIM)
        bm = bm.reshape(bsz, length, MB_GROUPS, MB_STATE)
        cm = cm.reshape(bsz, length, MB_GROUPS, MB_STATE)
        per_dir = []
        for d, dt_raw in enumerate((dt_f, dt_b)):
            dt = jax.nn.softplus(dt_raw.astype(f32) + dt_bias[d].astype(f32))
            dt = dt.reshape(bsz, length, MB_GROUPS, MB_HPG)
            a = -jnp.exp(a_log[d].astype(f32)).reshape(MB_GROUPS, MB_HPG)
            per_dir.append((xs * dt[..., None], dt * a, bm, cm))
        return z, xs, per_dir

    zc, xsc, dirc = project(hc)
    zl, xsl, dirl = project(hl)
    s0 = jnp.zeros((hl.shape[0], MB_GROUPS, MB_HPG, MB_HEADDIM, MB_STATE), f32)
    yc_f, yl_f = two_pass(ssd_chunk_scan, dirc[0], dirl[0], s0, False)
    yc_b, yl_b = two_pass(ssd_chunk_scan, dirc[1], dirl[1], s0, True)

    def finish(y, xs, z):
        bsz, length = y.shape[:2]
        y = y + xs * d_skip.astype(f32).reshape(MB_GROUPS, MB_HPG, 1)
        y = y.reshape(bsz, length, MB_INNER) * jax.nn.silu(z.astype(f32))
        yg = y.reshape(bsz, length, MB_GROUPS, MB_INNER // MB_GROUPS)
        yg = yg * lax.rsqrt(jnp.mean(yg * yg, axis=-1, keepdims=True) + NORM_EPS)
        y = yg.reshape(bsz, length, MB_INNER) * norm_g
        return y.astype(z.dtype) @ w_out

    y_ctx = finish(yc_f + yc_b, xsc, zc) if need_ctx else None
    return y_ctx, finish(yl_f + yl_b, xsl, zl)

def setup_inputs(seed: int = 0) -> dict:
    key = jax.random.key(seed)
    keys = iter(jax.random.split(key, 48))
    f32 = jnp.float32
    d = D_MODEL

    def normal(shape, scale=1.0):
        return jax.random.normal(next(keys), shape, f32) * scale

    def dense_w(shape, fan_in, gain=1.0):
        return normal(shape, gain * fan_in ** -0.5)

    def unif(shape, lo, hi):
        return jax.random.uniform(next(keys), shape, f32, lo, hi)

    def norm_gain(shape):
        return 1.0 + normal(shape, 0.05)

    inputs = {}
    inputs['x'] = normal((BATCH, SEQ, d))
    inputs['c'] = normal((BATCH, d))
    inputs['ctx'] = normal((BATCH, CTX_LEN, d))
    inputs['c_ctx'] = normal((d,))
    inputs['mod_w'] = dense_w((DEPTH, d, 6 * d), d, 0.5)
    inputs['mod_b'] = normal((DEPTH, 6 * d), 0.02)
    inputs['norm_g'] = norm_gain((DEPTH, 4, d))
    inputs['gla_w_in'] = dense_w((N_GLA, d, GLA_IN), d)
    inputs['gla_w_g2'] = dense_w((N_GLA, 2, GLA_RANK, GLA_KEY), GLA_RANK)
    inputs['gla_b_g'] = normal((N_GLA, 2, GLA_KEY), 0.5)
    inputs['gla_norm_g'] = norm_gain((N_GLA, GLA_DV))
    inputs['gla_w_out'] = dense_w((N_GLA, GLA_VAL, d), GLA_VAL)
    inputs['rw_mu'] = unif((N_RWKV, 6, d), 0.0, 1.0)
    inputs['rw_w_rkv'] = dense_w((N_RWKV, 3, d, d), d)
    inputs['rw_w_o'] = dense_w((N_RWKV, d, d), d)
    inputs['rw_w0'] = unif((N_RWKV, 2, d), -6.0, 1.0)
    inputs['rw_w1'] = dense_w((N_RWKV, 2, d, RW_DECAY_LORA), d)
    inputs['rw_w2'] = dense_w((N_RWKV, 2, RW_DECAY_LORA, d), RW_DECAY_LORA, 0.5)
    inputs['rw_a0'] = normal((N_RWKV, 2, d), 0.1)
    inputs['rw_a1'] = dense_w((N_RWKV, 2, d, RW_A_LORA), d)
    inputs['rw_a2'] = dense_w((N_RWKV, 2, RW_A_LORA, d), RW_A_LORA, 0.5)
    inputs['rw_g1'] = dense_w((N_RWKV, d, RW_G_LORA), d)
    inputs['rw_g2'] = dense_w((N_RWKV, RW_G_LORA, d), RW_G_LORA)
    inputs['rw_k_k'] = 0.85 + normal((N_RWKV, d), 0.05)
    inputs['rw_k_a'] = 1.0 + normal((N_RWKV, d), 0.05)
    inputs['rw_r_k'] = normal((N_RWKV, RW_HEADS, RW_HEAD), 0.1)
    inputs['rw_ln_g'] = norm_gain((N_RWKV, d))
    inputs['rw_ln_b'] = normal((N_RWKV, d), 0.02)
    inputs['mb_w_in'] = dense_w((N_MAMBA, d, MB_IN), d)
    inputs['mb_conv_w'] = dense_w((N_MAMBA, MB_CONV_W, MB_CONV_CH), MB_CONV_W)
    inputs['mb_conv_b'] = normal((N_MAMBA, MB_CONV_CH), 0.02)
    dt = jnp.exp(unif((N_MAMBA, 2, MB_HEADS), math.log(1e-3), math.log(1e-1)))
    inputs['mb_dt_bias'] = dt + jnp.log(-jnp.expm1(-dt))
    inputs['mb_a_log'] = jnp.log(unif((N_MAMBA, 2, MB_HEADS), 1.0, 16.0))
    inputs['mb_d'] = 1.0 + normal((N_MAMBA, MB_HEADS), 0.1)
    inputs['mb_norm_g'] = norm_gain((N_MAMBA, MB_INNER))
    inputs['mb_w_out'] = dense_w((N_MAMBA, MB_INNER, d), MB_INNER)
    inputs['ff_w_gu'] = dense_w((N_DENSE, d, 2 * D_FF), d)
    inputs['ff_w_d'] = dense_w((N_DENSE, D_FF, d), D_FF)
    inputs['moe_router'] = dense_w((N_MOE, d, N_EXPERTS), d)
    inputs['moe_w_gu'] = dense_w((N_MOE, N_EXPERTS, d, 2 * D_FF_EXPERT), d)
    inputs['moe_w_d'] = dense_w((N_MOE, N_EXPERTS, D_FF_EXPERT, d), D_FF_EXPERT)
    return inputs

def reference(x, c, ctx, c_ctx, mod_w, mod_b, norm_g,
              gla_w_in, gla_w_g2, gla_b_g, gla_norm_g, gla_w_out,
              rw_mu, rw_w_rkv, rw_w_o, rw_w0, rw_w1, rw_w2, rw_a0, rw_a1, rw_a2, rw_g1, rw_g2,
              rw_k_k, rw_k_a, rw_r_k, rw_ln_g, rw_ln_b,
              mb_w_in, mb_conv_w, mb_conv_b, mb_dt_bias, mb_a_log, mb_d, mb_norm_g, mb_w_out,
              ff_w_gu, ff_w_d, moe_router, moe_w_gu, moe_w_d):
    rows = x.shape[1] // GRID_W
    x_lat, x_ctx = x, ctx
    for i in range(DEPTH):
        last = i == DEPTH - 1
        m_lat = jnp.split((jax.nn.silu(c) @ mod_w[i] + mod_b[i])[:, None, :], 6, axis=-1)
        m_ctx = jnp.split((jax.nn.silu(c_ctx) @ mod_w[i] + mod_b[i])[None, None, :], 6, axis=-1)
        h_lat = modulate(x_lat, norm_g[i, 0], m_lat[0], m_lat[1])
        h_ctx = modulate(x_ctx, norm_g[i, 0], m_ctx[0], m_ctx[1])
        kind, j = i % N_MIXERS, i // N_MIXERS
        if kind == 0:
            y_ctx, y_lat = gla_mixer(h_ctx, h_lat, gla_w_in[j], gla_w_g2[j], gla_b_g[j], gla_norm_g[j],
                                     gla_w_out[j], not last)
        elif kind == 1:
            y_ctx, y_lat = rwkv_mixer(h_ctx, h_lat, rows, rw_mu[j], rw_w_rkv[j], rw_w_o[j], rw_w0[j], rw_w1[j],
                                      rw_w2[j], rw_a0[j], rw_a1[j], rw_a2[j], rw_g1[j], rw_g2[j], rw_k_k[j],
                                      rw_k_a[j], rw_r_k[j], rw_ln_g[j], rw_ln_b[j], not last)
        else:
            y_ctx, y_lat = mamba_mixer(h_ctx, h_lat, mb_w_in[j], mb_conv_w[j], mb_conv_b[j], mb_dt_bias[j],
                                       mb_a_log[j], mb_d[j], mb_norm_g[j], mb_w_out[j], not last)
        if i % 2 == 0:
            ffn = functools.partial(swiglu, w_gu=ff_w_gu[i // 2], w_d=ff_w_d[i // 2])
        else:
            ffn = functools.partial(moe_ffn, router=moe_router[i // 2], w_gu=moe_w_gu[i // 2],
                                    w_d=moe_w_d[i // 2])
        x_lat = x_lat + m_lat[2] * rmsnorm(y_lat, norm_g[i, 1])
        x_lat = x_lat + m_lat[5] * rmsnorm(ffn(modulate(x_lat, norm_g[i, 2], m_lat[3], m_lat[4])), norm_g[i, 3])
        if not last:
            x_ctx = x_ctx + m_ctx[2] * rmsnorm(y_ctx, norm_g[i, 1])
            x_ctx = x_ctx + m_ctx[5] * rmsnorm(ffn(modulate(x_ctx, norm_g[i, 2], m_ctx[3], m_ctx[4])),
                                               norm_g[i, 3])
    return x_lat


_drawn_inputs = setup_inputs


def setup_inputs(seed=0):
    import zlib

    import numpy as np

    out = dict(_drawn_inputs(seed))
    spreads = {}
    factors = {'rw_w1': 3.197, 'rw_w2': 4.4, 'rw_a0': 2.896, 'rw_ln_g': 3.059, 'rw_ln_b': 6.335}
    for name, (base, spread) in spreads.items():
        noise = np.random.default_rng([zlib.crc32(name.encode()), seed]).standard_normal(out[name].shape)
        drawn = base * np.exp(spread * noise) if base else spread * noise
        out[name] = jnp.asarray(drawn.astype(out[name].dtype))
    for name, factor in factors.items():
        out[name] = (out[name] * factor).astype(out[name].dtype)
    return out
```

```python
import concourse.bass as bass
from concourse import mybir
from contextlib import ExitStack

import numpy as np

F32 = mybir.dt.float32
ALU = mybir.AluOpType
ACT = mybir.ActivationFunctionType
AX = mybir.AxisListType

P = 128
D = 1024
KT = D // P
SEG = 256
TOK = 2 * SEG
CH = 64
NCH = TOK // CH
EPS = 1e-6

GH, GDK, GDV, GRANK = 4, 128, 256, 16
GKEY, GVAL = GH * GDK, GH * GDV
DFF = 2816
FT = DFF // P

RING = 6
SLOT = 2048

PACKS = [[("mod_b", 96), ("c", 8), ("c_ctx", 8), ("gla_b_g", 8), ("gla_norm_g", 2)],
         [("norm_g", 64), ("rw_mu", 48), ("rw_w0", 16)],
         [("rw_a0", 16), ("rw_k_k", 8), ("rw_k_a", 8), ("rw_r_k", 8), ("rw_ln_g", 8), ("rw_ln_b", 8)]]
VEC = {}
for _n, _pack in enumerate(PACKS):
    _row = 0
    for _name, _rows in _pack:
        VEC[_name] = _n * P + _row
        _row += _rows

HP = D // P
SC = SEG // CH
GW = 64
GRK = 160
DECAY = float(np.exp(-0.5))
N_MASKS = 2 * (5 + 6 * 2 * 2)
NE, FE = 8, 3584
UNITS = FE // 512 * 4 + FE // SEG
assert UNITS % RING == 0



def hybrid_backbone(nc, A, out):
    ctx = ExitStack()
    with ctx:
        def sb(name, cols):
            return ctx.enter_context(nc.sbuf_tensor(name, [P, cols], F32))

        def sem(name):
            return ctx.enter_context(nc.semaphore(name))

        X = sb("x_stream", KT * TOK)[:, :].rearrange("p (k t) -> p k t", k=KT)
        ring = sb("weight_ring", RING * SLOT)
        vecs = sb("vecs", 3 * P)
        mods = sb("mods", 2 * 96)
        totals = sb("totals", NCH)
        gain = sb("gain", 2 * 4 * 16)
        csil = sb("csil", 16)
        ident = sb("ident", P)
        ones = sb("ones", P)
        chunk_reset = sb("chunk_reset", TOK)
        masks2 = sb("masks2", 2 * P)
        mask_fwd, mask_bwd = masks2[:, 0:P], masks2[:, P:2 * P]
        sq = sb("sq", 2 * TOK)
        std = sb("std", TOK)
        rstd = sb("rstd", TOK)
        ntmp = sb("ntmp", 2 * TOK)
        ARENA = 32000
        arena = sb("arena", ARENA)
        ps = [ctx.enter_context(nc.psum_tensor(f"bank{i}", [P, 512], F32)) for i in range(8)]

        def at(off, *dims):
            n = 1
            for d in dims:
                n *= d
            assert off + n <= ARENA, (off, n)
            v = arena[:, off:off + n]
            if len(dims) == 2:
                return v.rearrange("p (a b) -> p a b", a=dims[0])
            if len(dims) == 3:
                return v.rearrange("p (a b c) -> p a b c", a=dims[0], b=dims[1])
            return v

        x_tm = at(0, 4, D)
        packs = at(4096, 3, P)
        H = at(0, KT, TOK)
        Y1 = at(0, KT, TOK)
        Q = at(4096, GH, TOK)
        K = at(6144, GH, TOK)
        V = at(8192, 4, GVAL)
        O1 = at(8192, KT, TOK)
        R = at(12288, KT, TOK)
        GL = at(16384, TOK)
        LA = at(16896, GH, TOK)
        E = at(18944, GH, TOK)
        QF = at(20992, GH, TOK)
        KF = at(23040, GH, TOK)
        KDT = [at(25088 + 2048 * d, 4, GKEY) for d in range(2)]
        DEC = [at(29184 + 32 * d, GH, NCH) for d in range(2)]
        W2 = at(29248, 2, GKEY)
        ATT = at(18944, 2, TOK)
        ATB = at(19968, TOK)
        ST = at(20480, 2, GDV)
        KC = at(29248, GH, TOK)
        QD, KI = [QF, Q], [KF, K]
        H2 = at(0, KT, TOK)
        HID = at(4096, FT, TOK)
        SIL = at(15360, 4, TOK)
        O2 = at(17408, KT, TOK)

        KK, KEY = at(0, SC, HP, CH), at(2048, SC, HP, CH)
        AA = [at(4096 + 2048 * d, SC, HP, CH) for d in range(2)]
        SG = [at(8192 + 2048 * d, SC, HP, CH) for d in range(2)]
        VT = at(12288, SC, HP, CH)
        RR = at(14336, SC, HP, CH)
        YY = at(16384, SC, HP, CH)
        XX = at(16384, KT, SEG)
        HS = at(18432, KT, SEG)
        XJ = [at(20480 + 2048 * n, KT, SEG) for n in range(2)]
        WL, AL = at(24576, SEG), at(24832, SEG)
        LW1, LA1, LG1 = at(25088, KT, P), at(26112, KT, P), at(27136, KT, GRK)
        LW2, LA2 = at(28416, D), at(29440, D)
        G1 = at(30464, SEG)
        G2 = masks2[0:GRK - P, 0:SEG]
        LM = [[at(30720 + 64 * (2 * m + q), CH) for q in range(2)] for m in range(6)]
        STRICT = [at(30720 + 64 * (12 + q), CH) for q in range(2)]
        INCL = [at(30720 + 64 * (14 + q), CH) for q in range(2)]
        EYE2 = at(30720 + 64 * 16, CH)
        HEAD_ONES = at(31808, P)
        PC = [at(31936 + 8 * d, HP) for d in range(2)]
        KAM = at(31952, HP)
        spare = [at(18432 + 512 * n, HP, CH) for n in range(22)]
        spare += [X[:, :, CH * n:CH * n + CH] for n in (2, 3)]
        spare += [b[:, 512 * n:512 * n + 512].rearrange("p (a b) -> p a b", a=HP) for b, m in
                  ((sq, 2), (ntmp, 2), (std, 1), (rstd, 1)) for n in range(m)]
        WORK = []
        for d in range(2):
            names = "NT A R B K Bt Kt Vt NTl Lak Mrb Mrk T TT X".split()
            WORK.append({n: spare[2 * q + d] for q, n in enumerate(names)})
            WORK[d].update(W=WORK[d]["T"], SA=WORK[d]["NTl"])
            WORK[d]["ST"] = X[:, :, CH * d:CH * d + CH]
        U1 = at(4096, SC, HP, CH)
        GW2A, GW2B = at(18432, D), at(19456, D)
        O3 = at(20480, KT, SEG)
        H3 = at(0, KT, SEG)
        HTM = at(2048, 2, D)
        XG = at(4096, KT, P)
        HX = at(5120, FE // P, P)
        SX = at(8704, 2, 512)
        HH = at(9728, 2, 512)
        YS = at(10752, D)
        PG = at(11776, 2, P)
        PW = at(12032, 2, P)
        PWT = at(12288, SEG)
        YA = at(12544, KT, SEG)
        RT = at(14592, KT, NE)
        LOG = at(14656, 2, NE)
        SEL, CMB, RK0, RK1, EXL = (at(14672 + 16 * n, 2, NE) for n in range(5))
        GT, EQ = at(14752, 2, NE, NE), at(14880, 2, NE, NE)
        TRI = at(15008, NE, NE)
        SLOTS = at(15072, P)
        BEFORE = at(15200, P)
        MX = at(15328, 2)
        MORE = at(15330, 3 * NE)
        OT = at(15360, 2, D)
        more_i = at(17408, 2 * NE + 1).bitcast(mybir.dt.int32)

        S = {n: sem(n) for n in (
            "x_in vec_in small_in consts zeroed "
            "ff_mm x_t x_t_out vec_t vec_out csil mod_mm mod_out "
            "sq_ready sq_used std_ready nt_ready h_ready post_done "
            "pj pj_out gla_prep_v gla_prep_s kd_t kd_t_out "
            "att att_out att_m yin sup sup_out snew sinter y_out fn_sq fn_ss fn_std fn_done "
            "ff_a ff_b ff_sil ff_hid ffd ffd_out "
            "rw_small shift_ready mix_ready mix_used hid_mm hid_out z_mm z_out k_sq kn_mm kn_max kn_sqrt kn_rcp kn_done proj_done masks1 "
            "st_zero u_ready b_mm b_out mean_mm mean_sub var_sq var_mm var_std yn gate_mm gate_out o_in "
            "h_tm h_tm_out rt_in logits ex_in ex_out sel pos route pg xg xg_out ab sil hh tr tr_out yd yd_out sc sc_out moe_w "
            "v_chain s_chain p_chain out_t out_c stored").split()}
        def mod(layer, j, k, sg):
            c = 96 * layer + 2 * (8 * j + k) + (1 - sg)
            return mods[:, c:c + 1]

        def pre_gain(layer, sub, k, sg):
            c = (layer * 4 + 2 * sub) * 16 + 2 * k + (1 - sg)
            return gain[:, c:c + 1]

        def post_gain(layer, sub, k, sg):
            c = (layer * 4 + 2 * sub + 1) * 16 + 2 * k + (1 - sg)
            return gain[:, c:c + 1]

        def second_items(eng, item):
            eng.wait_ge(S["route"], 1)
            with eng.Fori(0, NE) as e:
                over = eng.value_load(more_i[0:1, bass.ds(e, 1)], min_val=0, max_val=1)
                n = eng.value_load(more_i[0:1, bass.ds(e + NE, 1)], min_val=NE, max_val=2 * NE)
                with eng.If(over > 0):
                    item(e, n)
            return eng.value_load(more_i[0:1, 2 * NE:2 * NE + 1], min_val=NE, max_val=2 * NE)

        def by_chunk(bank):
            return bank[:, 0:SEG].rearrange("p (c t) -> p c t", c=SC)

        def tok_cols(sg):
            return slice(SEG * sg, SEG * sg + SEG)

        pe_s = [sem(f"scan_pe{d}") for d in range(2)]
        dv_s = [sem(f"scan_dve{d}") for d in range(2)]
        ac_s = [sem(f"scan_act{d}") for d in range(2)]
        w_in = [sem(f"w_in{i}") for i in range(RING)]
        scan_open = sem("scan_open")
        N_SMALL = 2

        def cols256(w, n, width=256):
            v = w.rearrange("(k p) n -> p k n", p=P)
            return [v[:, :, i * 256:i * 256 + width] for i in range(n)]
        chunks, frees, first = [], [], {}

        def stream(name, views, said, start, step):
            first[name] = len(chunks)
            for i, v in enumerate(views):
                chunks.append(v)
                frees.append((S[said], start + step * (i + 1)))
        stream("mod0", cols256(A["mod_w"][0], 24), "mod_mm", 0, 1)
        w_in_gla = A["gla_w_in"][0]
        stream("gla_k", cols256(w_in_gla[:, GKEY:2 * GKEY], 2), "pj", 0, 2)
        stream("gla_q", cols256(w_in_gla[:, 0:GKEY], 2), "pj", 4, 2)
        stream("gla_g", [w_in_gla.rearrange("(k p) n -> p k n", p=P)[:, :, 3072:3104]], "pj", 8, 1)
        stream("gla_v", cols256(w_in_gla[:, 1024:2048], 4), "pj", 13, 4)
        stream("gla_r", cols256(w_in_gla[:, 2048:3072], 4), "pj", 33, 2)
        stream("gla_o", cols256(A["gla_w_out"][0], 4), "pj", 41, 2)
        ffa, ffb = cols256(A["ff_w_gu"][0][:, 0:DFF], 11), cols256(A["ff_w_gu"][0][:, DFF:2 * DFF], 11)
        stream("ff_gu", [x for ab in zip(ffa, ffb) for x in ab], "ff_mm", 0, 2)
        stream("ff_d", [A["ff_w_d"][0].rearrange("(k p) n -> p k n", p=P)[:, 2 * i:2 * i + 2, :] for i in range(11)], "ffd", 0, 1)
        stream("mod1", cols256(A["mod_w"][1], 24), "mod_mm", 24, 1)
        rkv = A["rw_w_rkv"][0]
        PJ1 = [49, 49 + 50]
        PROJ_END = [49 + 50, 49 + 50 + 60]
        KEY_PJ = [p + 34 for p in PJ1]
        MIX_DONE = [PJ1[sg] + n for sg, ns in enumerate(((1, 18, 42, 50), (1, 18, 42, 50, 58, 60))) for n in ns]
        for sg in range(2):
            for n, name in ((1, "k"), (2, "v"), (0, "r"))[:2 + sg]:
                stream(f"rw_{name}{sg}", cols256(rkv[n], 4), "pj", PJ1[sg] + 34 + 8 * "kvr".index(name), 2)
        stream("rw_o", cols256(A["rw_w_o"][0], 4), "pj", PROJ_END[1], 2)
        cid_moe = len(chunks)

        levels = range(1, 6)
        PE_STEPS, DV_STEPS, AC_STEPS = [], [], []
        for lat in range(2):
            PE_STEPS.append(["NT", "N"] + ["Mrb"] * lat + ["Lak", "Bt", "Kt", "Vt"] + ["Mrk"] * lat
                            + [f"{n}{l}" for l in levels for n in ("X", "TX", "XT") if (n, l) != ("TX", 5)]
                            + ["W", "SA"] + ["y"] * lat + ["U"])
            DV_STEPS.append(["b", "bx", "A", "PC"] + ["R"] * lat + ["kka", "B", "t1", "t2", "t3", "K", "V", "T0", "T", "TT0", "TT"]
                            + ["NTl1"] + ["Mrb"] * lat + ["Lak"] + ["Mrk"] * lat
                            + [x for l in levels for x in ([f"T{l}"] if l < 5 else []) + [f"TT{l}"] + ([f"NTl{l + 1}"] if l < 5 else [])]
                            + ["y"] * lat + ["U", "ST"])
            AC_STEPS.append(["e1", "e2", "e3", "NT", "Bt", "Kt", "Vt"] + [f"X{l}" for l in levels] + ["W", "SA"])

        class Steps:

            def __init__(self, steps, sems):
                self.steps, self.sems = steps, sems

            def value(self, lat, i, name):
                n = len(self.steps[lat])
                return SC * len(self.steps[0]) * lat + i * n + self.steps[lat].index(name) + 1

            def before(self, lat, i):
                return SC * len(self.steps[0]) * lat + i * len(self.steps[lat])
        PES, DVS, ACS = Steps(PE_STEPS, pe_s), Steps(DV_STEPS, dv_s), Steps(AC_STEPS, ac_s)
        all_scanned = SC * (len(PE_STEPS[0]) + len(PE_STEPS[1]))

        def slot(cid, k):
            v = ring[:, (cid % RING) * SLOT:(cid % RING + 1) * SLOT]
            return v.rearrange("p (k n) -> p k n", k=k)

        def arrived(eng, cid):
            eng.wait_ge(w_in[cid % RING], 16 * (cid // RING + 1))

        block = ctx.enter_context(nc.Block())

        @block.sync
        def _(sp):
            for n, name in enumerate(("ctx", "x")):
                sp.dma_start(x_tm[:, 2 * n:2 * n + 2, :],
                             A[name][0].rearrange("(t p) d -> p t d", p=P)).then_inc(S["x_in"], 16)
            for n, pack in enumerate(PACKS):
                row = 0
                for name, rows in pack:
                    v = A[name]
                    while len(v.shape) > 2:
                        v = v.rearrange("a b ... -> (a b) ...")
                    if len(v.shape) == 2:
                        v = v.rearrange("a b -> (a b)")
                    sp.dma_start(packs[row:row + rows, n, :], v.rearrange("(r c) -> r c", c=P)).then_inc(S["vec_in"], 16)
                    row += rows
            for cid, src in enumerate(chunks):
                if cid >= RING:
                    sp.wait_ge(*frees[cid - RING])
                kk, cc = src.shape[1], src.shape[2]
                dst = ring[:, (cid % RING) * SLOT:(cid % RING) * SLOT + kk * cc].rearrange("p (k n) -> p k n", k=kk)
                sp.dma_start(dst, src).then_inc(w_in[cid % RING], 16)
                if cid == RING - 1:
                    sp.wait_ge(S["vec_out"], 3)
                    sp.wait_ge(S["x_t_out"], KT)
                    sp.wait_ge(S["zeroed"], 1)
                    for d in range(2):
                        sp.dma_start(W2[16 * d:16 * d + 16, d, :], A["gla_w_g2"][0, d]).then_inc(S["small_in"], 16)
            gu, wd = A["moe_w_gu"][0], A["moe_w_d"][0]

            def expert(e, n):
                u = 0
                for j in range(FE // 512):
                    for half in range(2):
                        for kh in range(2):
                            col = half * FE + 512 * j
                            src = gu[e, :, col:col + 512].rearrange("(k p) n -> p k n", p=P)[:, 4 * kh:4 * kh + 4, :]
                            sp.wait_ge(S["moe_w"], UNITS * n + u + 1)
                            sp.dma_start(slot(cid_moe + u, 4), src).then_inc(w_in[(cid_moe + u) % RING], 16)
                            u += 1
                for i in range(FE // SEG):
                    src = wd[e, SEG * i:SEG * i + SEG, :].rearrange("(k p) n -> p k n", p=P)
                    sp.wait_ge(S["moe_w"], UNITS * n + u + 1)
                    sp.dma_start(slot(cid_moe + u, 2), src).then_inc(w_in[(cid_moe + u) % RING], 16)
                    u += 1
            with sp.Fori(0, NE) as e:
                expert(e, e)
            second_items(sp, expert)
            sp.wait_ge(S["out_c"], 4)
            sp.dma_start(out[0].rearrange("(t p) d -> p t d", p=P), OT[:, :, :]).then_inc(S["stored"], 16)
            sp.wait_ge(S["stored"], 16)

        @block.gpsimd
        def _(pool):
            g = nc.gpsimd
            n = [0]

            def link(ins):
                n[0] += 1
                ins.then_inc(S["p_chain"], 1)
                pool.wait_ge(S["p_chain"], n[0])
            link(g.memset(ident[:, :], 0.0))
            g.affine_select(out=ident[:, :], in_=ident[:, :], compare_op=ALU.not_equal, fill=1.0, base=0,
                            pattern=[[-1, P]], channel_multiplier=1).then_inc(S["consts"], 1)
            g.memset(ones[:, :], 1.0).then_inc(S["consts"], 1)
            g.memset(totals[:, :], 0.0).then_inc(scan_open, 1)
            link(g.memset(chunk_reset[:, :], 1.0))
            g.memset(chunk_reset[:, ::CH], 0.0).then_inc(S["consts"], 1)
            link(g.memset(mask_fwd[:, :], 1.0))
            link(g.memset(mask_bwd[:, :], 1.0))
            link(g.memset(mask_fwd[CH:P, 0:CH], 0.0))
            link(g.memset(mask_bwd[0:CH, CH:P], 0.0))
            g.affine_select(out=mask_fwd[:, :], in_=mask_fwd[:, :], compare_op=ALU.is_ge, fill=0.0, base=0,
                            pattern=[[1, P]], channel_multiplier=-1).then_inc(S["consts"], 1)
            g.affine_select(out=mask_bwd[:, :], in_=mask_bwd[:, :], compare_op=ALU.is_ge, fill=0.0, base=0,
                            pattern=[[-1, P]], channel_multiplier=1).then_inc(S["consts"], 1)
            pool.wait_ge(S["consts"], 5)
            link(g.memset(mask_fwd[0:CH, CH:P], 0.0))
            g.memset(mask_bwd[CH:P, 0:CH], 0.0).then_inc(S["consts"], 1)
            pool.wait_ge(S["x_t"], KT)
            pool.wait_ge(S["vec_t"], 3)
            g.memset(W2[0:32, :, :], 0.0).then_inc(S["zeroed"], 1)

            pool.wait_ge(S["post_done"], KT)
            for q in range(2):
                rows = slice(CH * q, CH * q + CH)

                def select(v, op, base, mult, pattern):
                    g.affine_select(out=v[rows], in_=v[rows], compare_op=op, fill=0.0, base=base,
                                    pattern=pattern, channel_multiplier=mult).then_inc(S["masks1"], 1)
                    count[0] += 1
                    pool.wait_ge(S["masks1"], count[0])
                if q == 0:
                    count = [0]
                    for v in [x for m in LM for x in m] + STRICT + INCL + [EYE2]:
                        link(g.memset(v, 1.0))
                    link(g.memset(HEAD_ONES[:, :], 0.0))
                    link(g.memset(HEAD_ONES[0:CH, 0:CH], 1.0))
                    link(g.memset(HEAD_ONES[CH:P, CH:P], 1.0))
                select(STRICT[0], ALU.is_gt, 0, -1, [[1, CH]])
                select(STRICT[1], ALU.is_gt, 0, 1, [[-1, CH]])
                select(INCL[0], ALU.is_ge, 0, -1, [[1, CH]])
                select(INCL[1], ALU.is_ge, 0, 1, [[-1, CH]])
                select(EYE2, ALU.is_equal, 0, 1, [[-1, CH]])
                for m in range(6):
                    h, b, nb = 2 ** m, 2 ** (m + 1), CH // 2 ** (m + 1)
                    for w in range(2):
                        cols = LM[m][w].rearrange("p (n z) -> p n z", z=b)
                        link(g.memset(cols[rows, :, (0 if w == 0 else h):(h if w == 0 else b)], 0.0))
                        lo = h if w == 1 else 0
                        select(cols, ALU.is_ge, -lo, 1, [[-b, nb], [0, b]])
                        select(cols, ALU.is_ge, lo + h - 1, -1, [[b, nb], [0, b]])
            assert count[0] == N_MASKS
            for sg in range(2):
                if sg == 1:
                    for d in range(2):
                        pool.wait_ge(pe_s[d], PES.before(0, SC))
                        pool.wait_ge(dv_s[d], DVS.before(0, SC))
                for dst, src in ([(LW1[:, :, CH * d:CH * d + CH], A["rw_w1"][0, d].rearrange("(k p) n -> p k n", p=P)) for d in range(2)]
                                 + [(LA1[:, :, CH * d:CH * d + CH], A["rw_a1"][0, d].rearrange("(k p) n -> p k n", p=P)) for d in range(2)]
                                 + [(LG1[:, :, :], A["rw_g1"][0].rearrange("(k p) n -> p k n", p=P)),
                                    (LW2[:, :], A["rw_w2"][0].rearrange("a b n -> (a b) n")),
                                    (LA2[:, :], A["rw_a2"][0].rearrange("a b n -> (a b) n"))]):
                    pool.dma_start(dst, src).then_inc(S["rw_small"], 16)
            for d in range(2):
                pool.wait_ge(pe_s[d], all_scanned)
                pool.wait_ge(dv_s[d], DVS.before(1, SC))
            pool.dma_start(GW2A[:, :], A["rw_g2"][0, 0:P, :]).then_inc(S["rw_small"], 16)
            pool.dma_start(GW2B[0:GRK - P, :], A["rw_g2"][0, P:GRK, :]).then_inc(S["rw_small"], 16)
            pool.wait_ge(S["post_done"], 3 * KT)
            pool.dma_start(RT[:, :, :], A["moe_router"][0].rearrange("(k p) n -> p k n", p=P)).then_inc(S["rt_in"], 16)
            link(g.memset(TRI[:, :, :], 1.0))
            link(g.memset(BEFORE[:, :], 1.0))
            link(g.memset(YA[:, :, :], 0.0))
            g.affine_select(out=TRI[:, :, :], in_=TRI[:, :, :], compare_op=ALU.is_gt, fill=0.0, base=0,
                            pattern=[[1, NE], [-1, NE]], channel_multiplier=0).then_inc(S["consts"], 1)
            g.affine_select(out=BEFORE[:, :], in_=BEFORE[:, :], compare_op=ALU.is_gt, fill=0.0, base=0,
                            pattern=[[1, P]], channel_multiplier=-1).then_inc(S["consts"], 1)
            g.iota(SLOTS[:, :], pattern=[[1, P]], base=0, channel_multiplier=0, allow_small_or_imprecise_dtypes=True).then_inc(S["consts"], 1)

        @block.tensor
        def _(pe):
            T = nc.tensor

            def norm_stats(n, width):
                for k in range(KT):
                    pe.wait_ge(S["sq_ready"], KT * n + k + 1)
                    T.matmul(ps[7][:, 0:width], ones[:, :], sq[:, (k % 2) * TOK:(k % 2) * TOK + width],
                             start=(k == 0), stop=(k == KT - 1)).then_inc(S["sq_used"], 1)

            pe.wait_ge(S["consts"], 6)
            pe.wait_ge(S["vec_in"], 16 * sum(len(p) for p in PACKS))
            for n, pack in enumerate(PACKS):
                rows = sum(r for _, r in pack)
                T.transpose(ps[6][:, n * P:n * P + rows], packs[0:rows, n, :], ident[0:rows, 0:rows]).then_inc(S["vec_t"], 1)
            pe.wait_ge(S["x_in"], 32)
            for k in range(KT):
                if k >= 6:
                    pe.wait_ge(S["x_t_out"], k - 5)
                for t in range(4):
                    ins = T.transpose(ps[k % 6][:, t * P:t * P + P], x_tm[:, t, k * P:k * P + P], ident[:, :])
                ins.then_inc(S["x_t"], 1)

            def modulation(layer):
                cid = first[f"mod{layer}"]
                for i in range(24):
                    arrived(pe, cid + i)
                    w = slot(cid + i, KT)
                    for j in range(2):
                        o = ps[6][:, 4 * i + 2 * j:4 * i + 2 * j + 2]
                        for k in range(KT):
                            ins = T.matmul(o, w[:, k, j * P:j * P + P], csil[:, 2 * k:2 * k + 2],
                                           start=(k == 0), stop=(k == KT - 1))
                    ins.then_inc(S["mod_mm"], 1)

            pe.wait_ge(S["csil"], 2)
            modulation(0)
            norm_stats(0, TOK)

            tile = [0]

            def next_bank():
                n = tile[0]
                tile[0] += 1
                if n >= 6:
                    pe.wait_ge(S["pj_out"], n - 5)
                return ps[n % 6]

            def project(cid, src, width, n_chunks):
                for i in range(n_chunks):
                    arrived(pe, cid + i)
                    w = slot(cid + i, KT)
                    for j in range(2):
                        b = next_bank()
                        for k in range(KT):
                            ins = T.matmul(b[:, 0:width], w[:, k, j * P:j * P + P], src[:, k, :],
                                           start=(k == 0), stop=(k == KT - 1))
                        ins.then_inc(S["pj"], 1)

            for k in range(KT):
                pe.wait_ge(S["h_ready"], k + 1)
            project(first["gla_k"], H, TOK, 2)
            project(first["gla_q"], H, TOK, 2)
            cid = first["gla_g"]
            arrived(pe, cid)
            w = ring[:, (cid % RING) * SLOT:(cid % RING) * SLOT + 32 * KT].rearrange("p (k n) -> p k n", k=KT)
            b = next_bank()
            for k in range(KT):
                ins = T.matmul(b[0:32, :], w[:, k, :], H[:, k, :], start=(k == 0), stop=(k == KT - 1))
            ins.then_inc(S["pj"], 1)
            pe.wait_ge(S["pj_out"], 9)
            pe.wait_ge(S["small_in"], 32)

            def gate_tiles(d):
                for h in range(GH):
                    T.matmul(next_bank()[:, :], W2[0:32, d, h * P:h * P + P], GL[0:32, :],
                             start=True, stop=True).then_inc(S["pj"], 1)

            def keys_by_token(d):
                pe.wait_ge(S["gla_prep_v"], 5 * d + 5)
                for t in range(4):
                    n = 4 * d + t
                    if n >= 2:
                        pe.wait_ge(S["kd_t_out"], n - 1)
                    for h in range(GH):
                        ins = T.transpose(ps[6 + n % 2][:, h * P:h * P + P], E[:, h, t * P:t * P + P], ident[:, :])
                    ins.then_inc(S["kd_t"], 1)

            gate_tiles(0)
            for i in range(4):
                cid = first["gla_v"] + i
                arrived(pe, cid)
                w = slot(cid, KT)
                for t in range(4):
                    b = next_bank()
                    for k in range(KT):
                        ins = T.matmul(b[:, 0:256], H[:, k, t * P:t * P + P], w[:, k, :],
                                       start=(k == 0), stop=(k == KT - 1))
                    ins.then_inc(S["pj"], 1)
            keys_by_token(0)
            gate_tiles(1)
            project(first["gla_r"], H, TOK, 4)
            keys_by_token(1)
            pe.wait_ge(S["pj_out"], tile[0])
            pe.wait_ge(S["kd_t_out"], 8)

            for h in range(GH):
                if h >= 1:
                    pe.wait_ge(S["att_out"], 2 * h)
                for d in range(2):
                    for t in range(4):
                        ins = T.matmul(ps[d][:, t * P:t * P + P], KI[d][:, h, t * P:t * P + P],
                                       QD[d][:, h, t * P:t * P + P], start=True, stop=True)
                    ins.then_inc(S["att"], 1)
                pe.wait_ge(S["att_m"], h + 1)
                if h >= 1:
                    pe.wait_ge(S["y_out"], 2 * h)
                for vt in range(2):
                    for t in range(4):
                        T.matmul(ps[2 + vt][:, t * P:t * P + P], V[:, t, h * GDV + vt * P:h * GDV + vt * P + P],
                                 ATT[:, h % 2, t * P:t * P + P], start=(t == 0), stop=False, skip_group_check=True)
                for i in range(NCH):
                    for d in range(2):
                        if i < NCH - 1:
                            n = (NCH - 1) * h + i
                            if n >= 2:
                                pe.wait_ge(S["snew"], 2 * (n - 2) + d + 1)
                            c = i if d == 0 else (3 - i if i < 4 else 11 - i)
                            r0 = CH * (c % 2)
                            T.matmul(ps[4 + d + 2 * (n % 2)][:, 0:GDV],
                                     KDT[d][r0:r0 + CH, c // 2, h * P:h * P + P],
                                     V[r0:r0 + CH, c // 2, h * GDV:h * GDV + GDV],
                                     start=True, stop=True).then_inc(S["sup"], 1)
                    if i >= 1:
                        for d in range(2):
                            n = (NCH - 1) * h + i
                            c = i if d == 0 else (3 - i if i < 4 else 11 - i)
                            pe.wait_ge(S["snew"], 2 * (n - 1) + d + 1)
                            for vt in range(2):
                                ins = T.matmul(ps[2 + vt][:, c * CH:c * CH + CH], ST[:, d, vt * P:vt * P + P],
                                               QD[d][:, h, c * CH:c * CH + CH], start=False,
                                               stop=(i == NCH - 1 and d == 1), skip_group_check=True)
                            ins.then_inc(S["sinter"], 1)

            for h in range(GH):
                for vt in range(2):
                    pe.wait_ge(S["fn_sq"], 2 * h + vt + 1)
                    T.matmul(ps[h % 2][:, :], ones[:, :], sq[:, vt * TOK:vt * TOK + TOK],
                             start=(vt == 0), stop=(vt == 1)).then_inc(S["fn_ss"], 1)
            pe.wait_ge(S["fn_done"], KT)
            project(first["gla_o"], Y1, TOK, 4)
            norm_stats(1, TOK)
            norm_stats(2, TOK)

            for k in range(KT):
                pe.wait_ge(S["h_ready"], KT + k + 1)
            for p in range(FT // 2):
                for ab in range(2):
                    cid = first["ff_gu"] + 2 * p + ab
                    arrived(pe, cid)
                    w = slot(cid, KT)
                    if p >= 2 and ab == 0:
                        pe.wait_ge(S["ff_hid"], 2 * (p - 1))
                    for j in range(2):
                        for k in range(KT):
                            ins = T.matmul(ps[4 * (p % 2) + 2 * ab + j][:, :], w[:, k, j * P:j * P + P], H2[:, k, :],
                                           start=(k == 0), stop=(k == KT - 1))
                        ins.then_inc(S["ff_mm"], 1)
            pe.wait_ge(S["ff_hid"], FT)
            cid = first["ff_d"]
            for i in range(FT // 2):
                arrived(pe, cid + i)
                w = slot(cid + i, 2)
                for j in range(KT):
                    for k in range(2):
                        ins = T.matmul(ps[j][:, :], w[:, k, j * P:j * P + P], HID[:, 2 * i + k, :],
                                       start=(i == 0 and k == 0), stop=(i == FT // 2 - 1 and k == 1))
                ins.then_inc(S["ffd"], 1)
            pe.wait_ge(S["ffd_out"], KT)
            norm_stats(3, TOK)
            modulation(1)

            pe.wait_ge(S["masks1"], N_MASKS)
            pe.wait_ge(S["mod_out"], 2)
            jn = [0]

            def mix(sg):
                pe.wait_ge(S["mix_ready"], jn[0] + 1)
                jn[0] += 1
                return XJ[(jn[0] - 1) % 2]

            def hidden(w, cols, src):
                b = next_bank()
                for k in range(KT):
                    ins = T.matmul(b[0:cols, 0:SEG], w[:, k, :], src[:, k, :], start=(k == 0), stop=(k == KT - 1))
                ins.then_inc(S["pj"], 1)

            def segment(sg):
                norm_stats(4 + sg, SEG)
                pe.wait_ge(S["rw_small"], 16 * 7 * (sg + 1))
                for w1, w2, hid in ((LW1, LW2, WL), (LA1, LA2, AL)):
                    hidden(w1, P, mix(sg))
                    pe.wait_ge(S["pj_out"], tile[0])
                    for d in range(2):
                        for p in range(HP):
                            T.matmul(next_bank()[:, 0:SEG], w2[CH * d:CH * d + CH, p * P:p * P + P],
                                     hid[CH * d:CH * d + CH, :], start=True, stop=True).then_inc(S["pj"], 1)
                project(first[f"rw_k{sg}"], mix(sg), SEG, 4)
                for p in range(HP):
                    pe.wait_ge(S["k_sq"], HP * sg + p + 1)
                    if p >= 2 or sg:
                        pe.wait_ge(S["kn_max"], HP * sg + p - 1)
                    T.matmul(ps[6 + p % 2][:, 0:SEG], HEAD_ONES[:, :], sq[:, (p % 2) * TOK:(p % 2) * TOK + SEG],
                             start=True, stop=True).then_inc(S["kn_mm"], 1)
                project(first[f"rw_v{sg}"], mix(sg), SEG, 4)
                if sg:
                    project(first["rw_r1"], mix(sg), SEG, 4)
                    src = mix(sg)
                    hidden(LG1[:, :, 0:P], P, src)
                    hidden(LG1[:, :, P:GRK], GRK - P, src)
                pe.wait_ge(S["pj_out"], tile[0])
                pe.wait_ge(S["kn_done"], HP * (sg + 1))

            def scan(lat, i):
                bank = [ps[4 * d:4 * d + 4] for d in range(2)]
                rows = [slice(0, CH), slice(CH, P)]

                def heads(d, name, b, terms, need):
                    for c, n in need:
                        pe.wait_ge(c.sems[d], c.value(lat, i, n))
                    if need:
                        pe.wait_ge(scan_open, 1)
                    for p in range(HP):
                        for q, (lhs, rhs) in enumerate(terms):
                            for r in rows:
                                R_ = rhs[r, p, :] if rhs is not IDN else ident[r, r]
                                ins = T.matmul(bank[d][b][r, p * CH:p * CH + CH], lhs[r, p, :], R_,
                                               start=(q == 0), stop=(q == len(terms) - 1))
                    ins.then_inc(pe_s[d], 1)
                IDN = None
                both = range(2)
                w = WORK
                for d in both:
                    heads(d, "NT", 0, [(w[d]["B"], w[d]["A"])], [(DVS, "B")])
                    heads(d, "N", 1, [(w[d]["A"], w[d]["B"])], [])
                    if lat:
                        heads(d, "Mrb", 2, [(w[d]["B"], w[d]["R"])], [])
                for d in both:
                    c = i if d == 0 else SC - 1 - i
                    heads(d, "Lak", 3, [(w[d]["K"], w[d]["A"])], [(DVS, "K")])
                    heads(d, "Bt", 0, [(w[d]["B"], IDN)], [(ACS, "NT")])
                    heads(d, "Kt", 1, [(w[d]["K"], IDN)], [(DVS, "T0")])
                    heads(d, "Vt", 2, [(w[d]["X"], IDN)], [(DVS, "Mrb" if lat else "V")])
                    if lat:
                        heads(d, "Mrk", 3, [(w[d]["K"], w[d]["R"])], [(DVS, "Lak")])
                for l in levels:
                    for d in both:
                        heads(d, "X", 0, [(w[d]["NTl"], w[d]["T"])], [(DVS, f"NTl{l}"), (ACS, "Vt")])
                    for d in both:
                        if l < 5:
                            heads(d, "TX", 1, [(w[d]["TT"], w[d]["X"])], [(ACS, f"X{l}")])
                        heads(d, "XT", 2, [(w[d]["X"], w[d]["TT"])], [(ACS, f"X{l}")])
                for d in both:
                    pe.wait_ge(dv_s[d], DVS.before(lat, i))
                    heads(d, "W", 0, [(w[d]["A"], w[d]["ST"]), (w[d]["Lak"], w[d]["Vt"])], [(DVS, "TT5")])
                for d in both:
                    heads(d, "SA", 1, [(w[d]["TT"], w[d]["W"])], [(ACS, "W")])
                for d in both:
                    t_y = [(w[d]["ST"], w[d]["R"]), (w[d]["SA"], w[d]["Mrb"]), (w[d]["Vt"], w[d]["Mrk"])]
                    if lat:
                        heads(d, "y", 3, t_y, [(ACS, "SA")])
                    heads(d, "U", 2, [(w[d]["Bt"], w[d]["SA"]), (w[d]["Kt"], w[d]["Vt"])], [(ACS, "SA")])

            for sg in range(2):
                segment(sg)
                if sg == 0:
                    pe.wait_ge(S["st_zero"], 2)
                for i in range(SC):
                    scan(sg, i)
            for d in range(2):
                pe.wait_ge(dv_s[d], DVS.before(1, SC))
            for p in range(HP):
                pe.wait_ge(S["u_ready"], p + 1)
                if p >= 2:
                    pe.wait_ge(S["b_out"], p - 1)
                T.matmul(by_chunk(ps[p % 2]), HEAD_ONES[:, :], U1[:, :, p, :], start=True, stop=True).then_inc(S["b_mm"], 1)
            for p in range(HP):
                if p >= 2:
                    pe.wait_ge(S["mean_sub"], p - 1)
                T.matmul(by_chunk(ps[2 + p % 2]), HEAD_ONES[:, :], YY[:, :, p, :], start=True, stop=True).then_inc(S["mean_mm"], 1)
            pe.wait_ge(S["rw_small"], 16 * 16)
            for p in range(HP):
                pe.wait_ge(S["var_sq"], p + 1)
                if p >= 2:
                    pe.wait_ge(S["var_std"], p - 1)
                T.matmul(ps[4 + p % 2][:, 0:SEG], HEAD_ONES[:, :], sq[:, (p % 2) * TOK:(p % 2) * TOK + SEG],
                         start=True, stop=True).then_inc(S["var_mm"], 1)
                if p >= 2:
                    pe.wait_ge(S["o_in"], p - 1)
                T.matmul(ps[6 + p % 2][:, 0:SEG], GW2A[:, p * P:p * P + P], G1[:, :], start=True, stop=False)
                T.matmul(ps[6 + p % 2][:, 0:SEG], GW2B[0:GRK - P, p * P:p * P + P], G2, start=False,
                         stop=True).then_inc(S["gate_mm"], 1)
            pe.wait_ge(S["o_in"], HP)

            for i in range(4):
                arrived(pe, first["rw_o"] + i)
                w = slot(first["rw_o"] + i, KT)
                for j in range(2):
                    b = next_bank()
                    for k in range(KT):
                        ins = T.matmul(by_chunk(b), w[:, k, j * P:j * P + P], YY[:, :, k, :],
                                       start=(k == 0), stop=(k == KT - 1))
                    ins.then_inc(S["pj"], 1)
            pe.wait_ge(S["pj_out"], tile[0])
            norm_stats(6, SEG)
            norm_stats(7, SEG)

            pe.wait_ge(S["h_ready"], 5 * KT)
            pe.wait_ge(S["consts"], 9)
            for t in range(2):
                for q in range(2):
                    for k in range(4 * q, 4 * q + 4):
                        ins = T.transpose(ps[2 * t + q][:, (k % 4) * P:(k % 4) * P + P], H3[:, k, t * P:t * P + P], ident[:, :])
                    ins.then_inc(S["h_tm"], 1)
            pe.wait_ge(S["rt_in"], 16)
            for t in range(2):
                for k in range(KT):
                    ins = T.matmul(ps[4][:, t * NE:t * NE + NE], H3[:, k, t * P:t * P + P], RT[:, k, :],
                                   start=(k == 0), stop=(k == KT - 1))
            ins.then_inc(S["logits"], 1)
            pe.wait_ge(S["sel"], 1)
            T.matmul(ps[5][:, 0:NE], BEFORE[:, :], SEL[:, 0, :], start=True, stop=True)
            T.matmul(ps[5][:, NE:2 * NE], ones[:, :], SEL[:, 0, :], start=True, stop=False)
            T.matmul(ps[5][:, NE:2 * NE], BEFORE[:, :], SEL[:, 1, :], start=False, stop=True)
            for t in range(2):
                ins = T.matmul(ps[5][:, 2 * NE:3 * NE], ones[:, :], SEL[:, t, :], start=(t == 0), stop=(t == 1))
            ins.then_inc(S["pos"], 1)
            pe.wait_ge(S["h_tm_out"], 4)
            pe.wait_ge(S["route"], 1)
            T.transpose(ps[7][:, 0:P], ident[:, :], ident[:, :]).then_inc(S["moe_w"], RING)

            def unit(n, u, k):
                v = cid_moe + u
                pe.wait_ge(w_in[v % RING], 16 * (v // RING + 1) + 16 * (UNITS // RING) * n)
                return slot(v, k)

            def item(n):
                pe.wait_ge(S["pg"], 4 * n + 4)
                for q in range(2):
                    pe.wait_ge(S["tr_out"], 7 * n)
                    for k in range(4 * q, 4 * q + 4):
                        for t in range(2):
                            ins = T.matmul(ps[4 + q][:, (k % 4) * P:(k % 4) * P + P], HTM[:, t, k * P:k * P + P],
                                           PG[:, t, :], start=(t == 0), stop=(t == 1))
                    ins.then_inc(S["xg"], 1)
                pe.wait_ge(S["yd_out"], 2 * n)
                for t in range(2):
                    ins = T.transpose(ps[6][:, t * P:t * P + P], PW[:, t, :], ident[:, :])
                ins.then_inc(S["xg"], 1)
                pe.wait_ge(S["xg_out"], 3 * n + 3)
                pe.wait_ge(S["sc_out"], 4 * n)
                u = 0

                def turn(j):
                    pe.wait_ge(S["hh"], 7 * n + j + 1)
                    if j >= 2:
                        pe.wait_ge(S["tr_out"], 7 * n + j - 1)
                    for q in range(4):
                        ins = T.transpose(ps[4 + j % 2][:, q * P:q * P + P], HH[:, j % 2, q * P:q * P + P], ident[:, :])
                    ins.then_inc(S["tr"], 1)
                for j in range(7):
                    if j >= 2:
                        pe.wait_ge(S["hh"], 7 * n + j - 1)
                    for half in range(2):
                        for kh in range(2):
                            w = unit(n, u, 4)
                            for k in range(4):
                                kk = 4 * kh + k
                                ins = T.matmul(ps[2 * (j % 2) + half][:, :], XG[:, kk, :], w[:, k, :],
                                               start=(kk == 0), stop=(kk == KT - 1))
                            ins.then_inc(S["moe_w"], 1)
                            u += 1
                    if j >= 1:
                        turn(j - 1)
                turn(6)
                for i in range(FE // SEG):
                    w = unit(n, u, 2)
                    if i % 2 == 0:
                        pe.wait_ge(S["tr_out"], 7 * n + i // 2 + 1)
                    for k in range(2):
                        for h in range(2):
                            ins = T.matmul(ps[6 + h][:, :], HX[:, 2 * i + k, :], w[:, k, 512 * h:512 * h + 512],
                                           start=(i == 0 and k == 0), stop=(i == FE // SEG - 1 and k == 1))
                    ins.then_inc(S["moe_w"], 1)
                    u += 1
                pe.wait_ge(S["yd_out"], 2 * n + 2)
                for k in range(KT):
                    ins = T.matmul(ps[k // 2][:, (k % 2) * SEG:(k % 2) * SEG + SEG], YS[:, k * P:k * P + P], PWT[:, :],
                                   start=True, stop=True)
                    if k % 2:
                        ins.then_inc(S["sc"], 1)
            with pe.Fori(0, NE) as e:
                item(e)
            items = second_items(pe, lambda e, n: item(n))
            pe.wait_ge(S["sc_out"], 4 * items)
            norm_stats(8, SEG)
            pe.wait_ge(S["post_done"], 4 * KT)
            for t in range(2):
                for q in range(2):
                    for k in range(4 * q, 4 * q + 4):
                        ins = T.transpose(ps[2 * t + q][:, (k % 4) * P:(k % 4) * P + P],
                                          X[:, k, SEG + t * P:SEG + t * P + P], ident[:, :])
                    ins.then_inc(S["out_t"], 1)

        @block.scalar
        def _(act):
            C = nc.scalar
            n_link = [0]

            def link(ins):
                n_link[0] += 1
                ins.then_inc(S["s_chain"], 1)
                act.wait_ge(S["s_chain"], n_link[0])

            def norm_stats(n, src, width):
                for k in range(KT):
                    if KT * n + k >= 2:
                        act.wait_ge(S["sq_used"], KT * n + k - 1)
                    C.activation(sq[:, (k % 2) * TOK:(k % 2) * TOK + width], src[:, k, :], ACT.Square).then_inc(S["sq_ready"], 1)
                act.wait_ge(S["sq_used"], KT * n + KT)
                C.activation(std[:, 0:width], ps[7][:, 0:width], ACT.Sqrt, scale=1.0 / D, bias=EPS).then_inc(S["std_ready"], 1)

            def modulate(m, dst, layer, sub, segs):
                for k in range(KT):
                    act.wait_ge(S["nt_ready"], KT * m + k + 1)
                    for q, sg in enumerate(segs):
                        ins = C.activation(dst[:, k, q * SEG:(q + 1) * SEG],
                                           ntmp[:, (k % 2) * TOK + q * SEG:(k % 2) * TOK + (q + 1) * SEG], ACT.Identity,
                                           scale=pre_gain(layer, sub, k, sg), bias=mod(layer, 3 * sub, k, sg))
                    ins.then_inc(S["h_ready"], 1)

            for k in range(KT):
                act.wait_ge(S["x_t"], k + 1)
                C.copy(X[:, k, :], ps[k % 6][:, :]).then_inc(S["x_t_out"], 1)
            act.wait_ge(S["vec_out"], 3)
            for n, name in enumerate(("c", "c_ctx")):
                C.activation(csil[:, n::2], vecs[:, VEC[name]:VEC[name] + KT], ACT.Silu).then_inc(S["csil"], 1)
            act.wait_ge(S["x_t_out"], KT)
            norm_stats(0, X, TOK)
            act.wait_ge(S["mod_out"], 1)
            modulate(0, H, 0, 0, (0, 1))

            tile = [0]

            def empty(dst, func=ACT.Copy, rows=P, width=TOK, **kw):
                n = tile[0]
                tile[0] += 1
                act.wait_ge(S["pj"], n + 1)
                src = ps[n % 6][0:rows, 0:width]
                if len(dst.shape) == 3:
                    src = src.rearrange("p (c t) -> p c t", c=SC)
                C.activation(dst, src, func, **kw).then_inc(S["pj_out"], 1)
            for h in range(GH):
                empty(K[:, h, :])
            for h in range(GH):
                empty(Q[:, h, :], scale=float(GDK) ** -0.5)
            empty(GL[0:32, :], rows=32)

            def prep(d, between):
                if d == 1:
                    act.wait_ge(S["gla_prep_v"], 5)
                    act.wait_ge(S["kd_t"], 4)
                for h in range(GH):
                    col = VEC["gla_b_g"] + GH * d + h
                    empty(LA[:, h, :], ACT.Identity, bias=vecs[:, col:col + 1])
                act.wait_ge(S["pj_out"], tile[0])
                between(0)
                link(C.activation(E[:, :, :], LA[:, :, :], ACT.Abs))
                link(C.activation(E[:, :, :], E[:, :, :], ACT.Exp, scale=-1.0))
                C.activation(E[:, :, :], E[:, :, :], ACT.Ln, bias=1.0).then_inc(S["gla_prep_s"], 1)
                between(1)
                act.wait_ge(S["gla_prep_v"], 5 * d + 1)
                C.activation(E[:, :, :], LA[:, :, :], ACT.Exp, scale=1.0 / 16).then_inc(S["gla_prep_s"], 1)
                between(2)
                act.wait_ge(S["gla_prep_v"], 5 * d + 2)
                C.activation(E[:, :, :], LA[:, :, :], ACT.Exp, scale=-1.0 / 16).then_inc(S["gla_prep_s"], 1)
                between(3)
                act.wait_ge(S["gla_prep_v"], 5 * d + 4)
                C.activation(E[:, :, :], LA[:, :, :], ACT.Exp, scale=-1.0 / 16).then_inc(S["gla_prep_s"], 1)

            def empty_v(i):
                for t in range(4):
                    empty(V[:, t, i * 256:(i + 1) * 256], width=256)

            def empty_r(i):
                for k in (2 * i, 2 * i + 1):
                    empty(R[:, k, :], ACT.Silu)

            prep(0, empty_v)
            prep(1, empty_r)

            for h in range(GH):
                act.wait_ge(S["sinter"], 2 * (NCH - 1) * (h + 1))
                for vt in range(2):
                    C.copy(Y1[:, 2 * h + vt, :], ps[2 + vt][:, :]).then_inc(S["y_out"], 1)
            act.wait_ge(S["y_out"], 2 * GH)
            for h in range(GH):
                for vt in range(2):
                    if h >= 1:
                        act.wait_ge(S["fn_ss"], 2 * h)
                    C.activation(sq[:, vt * TOK:vt * TOK + TOK], Y1[:, 2 * h + vt, :], ACT.Square).then_inc(S["fn_sq"], 1)
                act.wait_ge(S["fn_ss"], 2 * h + 2)
                if h >= 1:
                    act.wait_ge(S["fn_done"], 2 * h)
                C.activation(std[:, :], ps[h % 2][:, :], ACT.Sqrt, scale=1.0 / GDV, bias=EPS).then_inc(S["fn_std"], 1)
            for k in range(KT):
                empty(O1[:, k, :])
            act.wait_ge(S["pj_out"], tile[0])
            norm_stats(1, O1, TOK)
            act.wait_ge(S["post_done"], KT)
            norm_stats(2, X, TOK)
            modulate(1, H2, 0, 1, (0, 1))
            for p in range(FT // 2):
                for j in range(2):
                    n = 2 * p + j
                    if p >= 2:
                        act.wait_ge(S["ff_hid"], n - 3)
                    act.wait_ge(S["ff_mm"], 4 * p + j + 1)
                    C.activation(SIL[:, n % 4, :], ps[4 * (p % 2) + j][:, :], ACT.Silu).then_inc(S["ff_sil"], 1)
            act.wait_ge(S["ffd"], FT // 2)
            for k in range(KT):
                C.copy(O2[:, k, :], ps[k][:, :]).then_inc(S["ffd_out"], 1)
            act.wait_ge(S["ffd_out"], KT)
            norm_stats(3, O2, TOK)

            def pairs(v, p):
                return v[:, :, p, :]

            def norm_root(sg, p):
                act.wait_ge(S["kn_max"], HP * sg + p + 1)
                q = slice((p % 2) * TOK, (p % 2) * TOK + SEG)
                C.activation(ntmp[:, q], ntmp[:, q], ACT.Sqrt).then_inc(S["kn_sqrt"], 1)

            def segment(sg):
                act.wait_ge(S["post_done"], 2 * KT)
                norm_stats(4 + sg, X[:, :, tok_cols(sg)], SEG)
                modulate(2 + sg, HS, 1, 0, (sg,))
                for hid, func, base, dst in ((WL, ACT.Tanh, "rw_w0", SG), (AL, ACT.Copy, "rw_a0", AA)):
                    empty(hid[:, :], func, width=SEG)
                    for d in range(2):
                        for p in range(HP):
                            col = VEC[base] + HP * d + p
                            empty(pairs(dst[d], p), ACT.Sigmoid, width=SEG, bias=vecs[:, col:col + 1])
                for p in range(HP):
                    n = tile[0]
                    act.wait_ge(S["pj"], n + 1)
                    if p >= 2:
                        act.wait_ge(S["kn_mm"], HP * sg + p - 1)
                    col = VEC["rw_k_k"] + p
                    C.activation(sq[:, (p % 2) * TOK:(p % 2) * TOK + SEG], ps[n % 6][:, 0:SEG], ACT.Square,
                                 scale=vecs[:, col:col + 1]).then_inc(S["k_sq"], 1)
                    empty(pairs(KEY, p), width=SEG)
                    if p >= 2:
                        norm_root(sg, p - 2)
                norm_root(sg, HP - 2)
                norm_root(sg, HP - 1)
                for p in range(HP):
                    empty(pairs(VT, p), width=SEG)
                if sg:
                    for p in range(HP):
                        empty(pairs(RR, p), width=SEG)
                    empty(G1[:, :], ACT.Sigmoid, width=SEG)
                    empty(G2, ACT.Sigmoid, rows=GRK - P, width=SEG)
                act.wait_ge(S["pj_out"], tile[0])
                act.wait_ge(S["kn_done"], HP * (sg + 1))

            def scan(lat, i):
                def step(d, dst, src, func, scale, need):
                    for c, n in need:
                        act.wait_ge(c.sems[d], c.value(lat, i, n))
                    C.activation(dst, src, func, scale=scale).then_inc(ac_s[d], 1)

                def bk(d, b):
                    return ps[4 * d + b][:, :].rearrange("p (a b) -> p a b", a=HP)
                w = WORK
                for d in range(2):
                    step(d, w[d]["NTl"], w[d]["TT"], ACT.Exp, -DECAY, [(DVS, "bx")])
                    step(d, w[d]["X"], w[d]["NT"], ACT.Exp, -DECAY, [(DVS, "b")])
                    step(d, w[d]["T"], w[d]["NT"], ACT.Exp, DECAY, [])
                for d in range(2):
                    step(d, w[d]["NT"], bk(d, 0), ACT.Copy, 1.0, [(PES, "NT"), (ACS, "e3")])
                for d in range(2):
                    step(d, w[d]["Bt"], bk(d, 0), ACT.Copy, 1.0, [(PES, "Bt")])
                    step(d, w[d]["Kt"], bk(d, 1), ACT.Copy, 1.0, [(PES, "Kt")])
                    step(d, w[d]["Vt"], bk(d, 2), ACT.Copy, 1.0, [(PES, "Vt")])
                for l in levels:
                    for d in range(2):
                        step(d, w[d]["X"], bk(d, 0), ACT.Copy, -1.0, [(PES, f"X{l}")])
                for d in range(2):
                    step(d, w[d]["W"], bk(d, 0), ACT.Copy, -1.0, [(PES, "W")])
                for d in range(2):
                    step(d, w[d]["SA"], bk(d, 1), ACT.Copy, 1.0, [(PES, "SA")])

            for sg in range(2):
                segment(sg)
                for i in range(SC):
                    scan(sg, i)
                for d in range(2):
                    act.wait_ge(dv_s[d], DVS.before(sg, SC))
            for p in range(HP):
                act.wait_ge(S["mean_sub"], p + 1)
                if p >= 2:
                    act.wait_ge(S["var_mm"], p - 1)
                C.activation(sq[:, (p % 2) * TOK:(p % 2) * TOK + SEG], pairs(YY, p), ACT.Square).then_inc(S["var_sq"], 1)
                act.wait_ge(S["var_mm"], p + 1)
                if p >= 1:
                    act.wait_ge(S["yn"], p)
                C.activation(std[:, 0:SEG], ps[4 + p % 2][:, 0:SEG], ACT.Sqrt, scale=1.0 / CH, bias=64e-5).then_inc(S["var_std"], 1)
            for k in range(KT):
                empty(O3[:, k, :], width=SEG)
            act.wait_ge(S["pj_out"], tile[0])
            norm_stats(6, O3, SEG)
            act.wait_ge(S["post_done"], 3 * KT)
            norm_stats(7, X[:, :, tok_cols(1)], SEG)
            modulate(4, H3, 1, 1, (1,))

            for n in range(4):
                act.wait_ge(S["h_tm"], n + 1)
                C.copy(HTM[:, n // 2, 512 * (n % 2):512 * (n % 2) + 512], ps[n][:, :]).then_inc(S["h_tm_out"], 1)
            act.wait_ge(S["ex_in"], 1)
            C.activation(EXL[:, :, :], EXL[:, :, :], ACT.Exp).then_inc(S["ex_out"], 1)

            def item(n):
                for q in range(2):
                    act.wait_ge(S["xg"], 3 * n + q + 1)
                    C.copy(XG[:, 4 * q:4 * q + 4, :], ps[4 + q][:, :].rearrange("p (a b) -> p a b", a=4)).then_inc(S["xg_out"], 1)
                act.wait_ge(S["xg"], 3 * n + 3)
                C.copy(PWT[:, :], ps[6][:, 0:SEG]).then_inc(S["xg_out"], 1)
                for j in range(8):
                    if j < 7:
                        act.wait_ge(S["moe_w"], RING + UNITS * n + 4 * j + 2)
                        if j >= 2:
                            act.wait_ge(S["hh"], 7 * n + j - 1)
                        C.activation(SX[:, j % 2, :], ps[2 * (j % 2)][:, :], ACT.Silu).then_inc(S["sil"], 1)
                    if j >= 1:
                        act.wait_ge(S["tr"], 7 * n + j)
                        C.copy(HX[:, 4 * (j - 1):4 * j, :], ps[4 + (j - 1) % 2][:, :].rearrange("p (a b) -> p a b", a=4))\
                            .then_inc(S["tr_out"], 1)
                act.wait_ge(S["moe_w"], RING + UNITS * (n + 1))
                for h in range(2):
                    C.copy(YS[:, 512 * h:512 * h + 512], ps[6 + h][:, :]).then_inc(S["yd_out"], 1)
            with act.Fori(0, NE) as e:
                item(e)
            items = second_items(act, lambda e, n: item(n))
            act.wait_ge(S["sc_out"], 4 * items)
            norm_stats(8, YA, SEG)
            for n in range(4):
                act.wait_ge(S["out_t"], n + 1)
                C.copy(OT[:, n // 2, 512 * (n % 2):512 * (n % 2) + 512], ps[n][:, :]).then_inc(S["out_c"], 1)

        @block.vector
        def _(dve):
            Vv = nc.vector
            n_link = [0]

            def link(ins):
                n_link[0] += 1
                ins.then_inc(S["v_chain"], 1)
                dve.wait_ge(S["v_chain"], n_link[0])

            def get_rstd(n, width, ready="std_ready"):
                dve.wait_ge(S[ready], n + 1)
                link(Vv.reciprocal(rstd[:, 0:width], std[:, 0:width]))

            def normalise(n, m, src, width):
                get_rstd(n, width)
                for k in range(KT):
                    if KT * m + k >= 2:
                        dve.wait_ge(S["h_ready"], KT * m + k - 1)
                    Vv.tensor_tensor(ntmp[:, (k % 2) * TOK:(k % 2) * TOK + width], src[:, k, :], rstd[:, 0:width],
                                     ALU.mult).then_inc(S["nt_ready"], 1)

            def post(n, src, width, layer, sub, segs):
                get_rstd(n, width)
                for k in range(KT):
                    link(Vv.tensor_tensor(src[:, k, :], src[:, k, :], rstd[:, 0:width], ALU.mult))
                    for q, sg in enumerate(segs):
                        cols = tok_cols(sg)
                        ins = Vv.scalar_tensor_tensor(X[:, k, cols], src[:, k, q * SEG:(q + 1) * SEG],
                                                      post_gain(layer, sub, k, sg), X[:, k, cols], ALU.mult, ALU.add)
                    ins.then_inc(S["post_done"], 1)
                    dve.wait_ge(S["post_done"], n_post[0] + k + 1)
                n_post[0] += KT
            n_post = [0]

            def gains(layer):
                dve.wait_ge(S["mod_mm"], 24 * (layer + 1))
                m = mods[:, 96 * layer:96 * layer + 96].rearrange("p (j s) -> p j s", s=2)
                b = VEC["mod_b"] + 48 * layer
                link(Vv.tensor_tensor(m, ps[6][:, 0:96].rearrange("p (j s) -> p j s", s=2),
                                      vecs[:, b:b + 48].unsqueeze(2).to_broadcast([P, 48, 2]), ALU.add))
                for sub in range(2):
                    g = VEC["norm_g"] + 32 * layer + 16 * sub
                    o = (layer * 4 + 2 * sub) * 16
                    pre = gain[:, o:o + 16].rearrange("p (k s) -> p k s", s=2)
                    pst = gain[:, o + 16:o + 32].rearrange("p (k s) -> p k s", s=2)
                    link(Vv.scalar_tensor_tensor(pre, m[:, 24 * sub + 8:24 * sub + 16, :], 1.0,
                                                 vecs[:, g:g + 8].unsqueeze(2).to_broadcast([P, 8, 2]), ALU.add, ALU.mult))
                    ins = (Vv.tensor_tensor(pst, m[:, 24 * sub + 16:24 * sub + 24, :],
                                          vecs[:, g + 8:g + 16].unsqueeze(2).to_broadcast([P, 8, 2]), ALU.mult))
                    if sub == 0:
                        link(ins)
                ins.then_inc(S["mod_out"], 1)
                dve.wait_ge(S["mod_out"], layer + 1)

            for n in range(3):
                rows = sum(r for _, r in PACKS[n])
                dve.wait_ge(S["vec_t"], 3)
                Vv.tensor_copy(vecs[:, n * P:n * P + rows], ps[6][:, n * P:n * P + rows]).then_inc(S["vec_out"], 1)
            dve.wait_ge(S["vec_out"], 3)
            gains(0)
            dve.wait_ge(S["x_t_out"], KT)
            normalise(0, 0, X, TOK)

            for d in range(2):
                dve.wait_ge(S["gla_prep_s"], 4 * d + 1)
                link(Vv.tensor_scalar_min(LA[:, :, :], LA[:, :, :], 0.0))
                link(Vv.tensor_tensor(LA[:, :, :], LA[:, :, :], E[:, :, :], ALU.subtract))
                for h in range(GH):
                    row = LA[:, h, :] if d == 0 else LA[:, h, ::-1]
                    ins = Vv.tensor_tensor_scan(row, chunk_reset[:, :], row, 0.0, ALU.mult, ALU.add)
                ins.then_inc(S["gla_prep_v"], 1)
                dve.wait_ge(S["gla_prep_v"], 5 * d + 1)
                dve.wait_ge(S["gla_prep_s"], 4 * d + 2)
                if d == 0:
                    dve.wait_ge(S["pj_out"], 8)
                last = CH - 1 if d == 0 else 0
                Ec = E[:, :, :].rearrange("p h (c t) -> p h c t", t=CH)
                link(Vv.tensor_copy(DEC[d][:, :, :], Ec[:, :, :, last]))
                Vv.tensor_tensor(QD[d][:, :, :], Q[:, :, :], E[:, :, :], ALU.mult).then_inc(S["gla_prep_v"], 1)
                dve.wait_ge(S["gla_prep_s"], 4 * d + 3)
                if d == 0:
                    Vv.tensor_tensor(KI[d][:, :, :], K[:, :, :], E[:, :, :], ALU.mult).then_inc(S["gla_prep_v"], 1)
                else:
                    link(Vv.tensor_copy(KC[:, :, :], K[:, :, :]))
                    Vv.tensor_tensor(KI[d][:, :, :], K[:, :, :], E[:, :, :], ALU.mult).then_inc(S["gla_prep_v"], 1)
                for h in range(GH):
                    L = LA[:, h, :].rearrange("p (c t) -> p c t", t=CH)
                    link(Vv.tensor_copy(totals[:, 0:NCH], L[:, :, last]))
                    ins = Vv.tensor_tensor(L, L, totals[:, 0:NCH].unsqueeze(2).to_broadcast([P, NCH, CH]), ALU.subtract)
                    if h < GH - 1:
                        link(ins)
                ins.then_inc(S["gla_prep_v"], 1)
                dve.wait_ge(S["gla_prep_s"], 4 * d + 4)
                Vv.tensor_tensor(E[:, :, :], (K if d == 0 else KC)[:, :, :], E[:, :, :], ALU.mult).then_inc(S["gla_prep_v"], 1)
                for t in range(4):
                    n = 4 * d + t
                    dve.wait_ge(S["kd_t"], n + 1)
                    Vv.tensor_copy(KDT[d][:, t, :], ps[6 + n % 2][:, :]).then_inc(S["kd_t_out"], 1)
            for h in range(GH):
                dve.wait_ge(S["att"], 2 * h + 1)
                if h >= 2:
                    dve.wait_ge(S["sinter"], 2 * (NCH - 1) * (h - 1))
                m4 = [m[:, :].unsqueeze(1).to_broadcast([P, 4, P]) for m in (mask_fwd, mask_bwd)]
                Vv.tensor_tensor(ATT[:, h % 2, :].rearrange("p (a b) -> p a b", a=4),
                                 ps[0][:, :].rearrange("p (a b) -> p a b", a=4), m4[0], ALU.mult).then_inc(S["att_out"], 1)
                dve.wait_ge(S["att"], 2 * h + 2)
                Vv.tensor_tensor(ATB[:, :].rearrange("p (a b) -> p a b", a=4),
                                 ps[1][:, :].rearrange("p (a b) -> p a b", a=4), m4[1], ALU.mult).then_inc(S["att_out"], 1)
                dve.wait_ge(S["att_out"], 2 * h + 2)
                Vv.tensor_tensor(ATT[:, h % 2, :], ATT[:, h % 2, :], ATB[:, :], ALU.add).then_inc(S["att_m"], 1)
                for i in range(NCH - 1):
                    for d in range(2):
                        n = (NCH - 1) * h + i
                        c = i if d == 0 else (3 - i if i < 4 else 11 - i)
                        dve.wait_ge(S["sup"], 2 * n + d + 1)
                        if n >= 1:
                            dve.wait_ge(S["sinter"], 2 * (n - 1) + d + 1)
                        upd = ps[4 + d + 2 * (n % 2)][:, 0:GDV]
                        if i == 0:
                            ins = Vv.tensor_copy(ST[:, d, :], upd)
                        else:
                            dve.wait_ge(S["snew"], 2 * (n - 1) + d + 1)
                            ins = Vv.scalar_tensor_tensor(ST[:, d, :], ST[:, d, :], DEC[d][:, h, c:c + 1], upd,
                                                          ALU.mult, ALU.add)
                        ins.then_inc(S["snew"], 1)
            for h in range(GH):
                get_rstd(h, TOK, "fn_std")
                for vt in range(2):
                    k = 2 * h + vt
                    g = VEC["gla_norm_g"] + vt
                    link(Vv.tensor_tensor(Y1[:, k, :], Y1[:, k, :], rstd[:, :], ALU.mult))
                    Vv.scalar_tensor_tensor(Y1[:, k, :], Y1[:, k, :], vecs[:, g:g + 1], R[:, k, :],
                                            ALU.mult, ALU.mult).then_inc(S["fn_done"], 1)
            post(1, O1, TOK, 0, 0, (0, 1))
            normalise(2, 1, X, TOK)
            for n in range(FT):
                p, j = n // 2, n % 2
                dve.wait_ge(S["ff_sil"], n + 1)
                dve.wait_ge(S["ff_mm"], 4 * p + 2 + j + 1)
                Vv.tensor_tensor(HID[:, n, :], SIL[:, n % 4, :], ps[4 * (p % 2) + 2 + j][:, :], ALU.mult).then_inc(S["ff_hid"], 1)
            post(3, O2, TOK, 0, 1, (0, 1))
            gains(1)

            jn = [0]

            def minus(out_, a, b):
                link(Vv.tensor_tensor(out_, a, b, ALU.subtract))

            def negated(out_, a):
                link(Vv.tensor_scalar(out_, a, -1.0, None, ALU.mult))

            def shift(sg):
                if sg == 0:
                    lo, hi = slice(0, KT // 2), slice(KT // 2, KT)
                    minus(XX[:, lo, 1:SEG], HS[:, lo, 0:SEG - 1], HS[:, lo, 1:SEG])
                    negated(XX[:, lo, 0:1], HS[:, lo, 0:1])
                    minus(XX[:, hi, 0:SEG - 1], HS[:, hi, 1:SEG], HS[:, hi, 0:SEG - 1])
                    negated(XX[:, hi, SEG - 1:SEG], HS[:, hi, SEG - 1:SEG])
                    return
                for k in range(4):
                    g, h = (v[:, k, :].rearrange("p (r c) -> p r c", c=GW) for v in (XX, HS))
                    if k < 2:
                        minus(g[:, :, 1:GW], h[:, :, 0:GW - 1], h[:, :, 1:GW])
                        negated(g[:, :, 0:1], h[:, :, 0:1])
                    else:
                        minus(g[:, :, 0:GW - 1], h[:, :, 1:GW], h[:, :, 0:GW - 1])
                        negated(g[:, :, GW - 1:GW], h[:, :, GW - 1:GW])
                minus(XX[:, 4:6, GW:SEG], HS[:, 4:6, 0:SEG - GW], HS[:, 4:6, GW:SEG])
                negated(XX[:, 4:6, 0:GW], HS[:, 4:6, 0:GW])
                minus(XX[:, 6:8, 0:SEG - GW], HS[:, 6:8, GW:SEG], HS[:, 6:8, 0:SEG - GW])
                negated(XX[:, 6:8, SEG - GW:SEG], HS[:, 6:8, SEG - GW:SEG])

            def segment(sg):
                normalise(4 + sg, 2 + sg, X[:, :, tok_cols(sg)], SEG)
                dve.wait_ge(S["h_ready"], KT * (3 + sg))
                shift(sg)
                for j in (1, 4, 2, 3, 0, 5)[:4 + 2 * sg]:
                    n = jn[0]
                    jn[0] += 1
                    if n >= 2:
                        dve.wait_ge(S["pj"], MIX_DONE[n - 2])
                    for k in range(KT):
                        col = VEC["rw_mu"] + KT * j + k
                        ins = Vv.scalar_tensor_tensor(XJ[n % 2][:, k, :], XX[:, k, :], vecs[:, col:col + 1], HS[:, k, :],
                                                      ALU.mult, ALU.add)
                    ins.then_inc(S["mix_ready"], 1)
                    if j == 3:
                        keys(sg)

            def keys(sg):
                if sg == 0:
                    link(Vv.tensor_scalar(KAM[:, :], vecs[:, VEC["rw_k_a"]:VEC["rw_k_a"] + HP], -1.0, 1.0, ALU.mult, ALU.add))
                for p in range(HP + 1):
                    if p < HP:
                        q = slice((p % 2) * TOK, (p % 2) * TOK + SEG)
                        dve.wait_ge(S["kn_mm"], HP * sg + p + 1)
                        if p >= 2:
                            dve.wait_ge(S["kn_rcp"], HP * sg + p - 1)
                        Vv.tensor_scalar(ntmp[:, q], ps[6 + p % 2][:, 0:SEG], 1e-24, None, ALU.max).then_inc(S["kn_max"], 1)
                    if p >= 1:
                        o = p - 1
                        q = slice((o % 2) * TOK, (o % 2) * TOK + SEG)
                        dve.wait_ge(S["kn_sqrt"], HP * sg + o + 1)
                        dve.wait_ge(S["kn_done"], HP * sg + o)
                        Vv.reciprocal(rstd[:, 0:SEG], ntmp[:, q]).then_inc(S["kn_rcp"], 1)
                        dve.wait_ge(S["kn_rcp"], HP * sg + o + 1)
                        dve.wait_ge(S["pj_out"], KEY_PJ[sg] + o + 1)
                        col = VEC["rw_k_k"] + o
                        Vv.scalar_tensor_tensor(KK[:, :, o, :], KEY[:, :, o, :], vecs[:, col:col + 1],
                                                rstd[:, 0:SEG].rearrange("p (c t) -> p c t", c=SC),
                                                ALU.mult, ALU.mult).then_inc(S["kn_done"], 1)

            def scan(lat, i):
                w = WORK

                def bk(d, b):
                    return ps[4 * d + b][:, :].rearrange("p (a b) -> p a b", a=HP)

                def over(v):
                    return v.unsqueeze(1).to_broadcast([P, HP, CH])

                def vec(v):
                    return v.unsqueeze(2).to_broadcast([P, HP, CH])

                def need(d, *what):
                    for c, n in what:
                        dve.wait_ge(c.sems[d], c.value(lat, i, n))
                    dve.wait_ge(dv_s[d], DVS.before(lat, i) + said[d])

                def said_one(d):
                    said[d] += 1
                said = [0, 0]

                def mult(d, dst, a, b, *what):
                    need(d, *what)
                    Vv.tensor_tensor(dst, a, b, ALU.mult).then_inc(dv_s[d], 1)
                    said_one(d)

                def add(d, dst, a, b, *what):
                    need(d, *what)
                    Vv.tensor_tensor(dst, a, b, ALU.add).then_inc(dv_s[d], 1)
                    said_one(d)
                ka = vecs[:, VEC["rw_k_a"]:VEC["rw_k_a"] + HP]
                chunk = [i, SC - 1 - i]

                def pick(v, d):
                    return v[:, bass.ds(chunk[d], 1), :, :].rearrange("p o a b -> p (o a) b")
                for d in range(2):
                    dve.wait_ge(pe_s[d], PES.before(lat, i))
                    dve.wait_ge(scan_open, 1)
                    sg_c = SG[d].rearrange("p c a b -> p c (a b)")[:, bass.ds(chunk[d], 1), :].rearrange("p o n -> p (o n)")
                    run = w[d]["NT"].rearrange("p a b -> p (a b)")
                    if d == 1:
                        sg_c, run = sg_c[:, ::-1], run[:, ::-1]
                    need(d)
                    Vv.tensor_tensor_scan(run, chunk_reset[:, :], sg_c, 0.0, ALU.mult, ALU.add).then_inc(dv_s[d], 1)
                    said_one(d)
                    need(d, (DVS, "b"))
                    Vv.tensor_tensor(w[d]["TT"], w[d]["NT"], pick(SG[d], d), ALU.subtract).then_inc(dv_s[d], 1)
                    said_one(d)
                for d in range(2):
                    last = CH - 1 if d == 0 else 0
                    mult(d, w[d]["A"], pick(KK, d), w[d]["NTl"], (ACS, "e1"))
                    need(d, (ACS, "e2"))
                    Vv.tensor_copy(PC[d], w[d]["X"][:, :, last]).then_inc(dv_s[d], 1)
                    said_one(d)
                    if lat:
                        mult(d, w[d]["R"], pick(RR, d), w[d]["X"])
                    mult(d, w[d]["NTl"], pick(KK, d), pick(AA[d], d), (DVS, "A"))
                    mult(d, w[d]["B"], w[d]["NTl"], w[d]["T"], (DVS, "kka"), (ACS, "e3"))
                    if lat:
                        need(d, (DVS, "R"))
                    mult(d, w[d]["TT"], pick(AA[d], d), vec(ka))
                    add(d, w[d]["TT"], w[d]["TT"], vec(KAM), (DVS, "t1"))
                    mult(d, w[d]["TT"], w[d]["TT"], pick(KEY, d), (DVS, "t2"))
                    mult(d, w[d]["K"], w[d]["TT"], w[d]["T"], (DVS, "t3"))
                    need(d, (DVS, "K"))
                    Vv.tensor_copy(w[d]["X"], pick(VT, d)).then_inc(dv_s[d], 1)
                    said_one(d)
                for d in range(2):
                    mult(d, w[d]["T"], bk(d, 1), over(LM[0][1 - d]), (PES, "N"), (DVS, "K"))
                    need(d, (DVS, "T0"))
                    Vv.tensor_tensor(w[d]["T"], over(EYE2), w[d]["T"], ALU.subtract).then_inc(dv_s[d], 1)
                    said_one(d)
                    mult(d, w[d]["TT"], w[d]["NT"], over(LM[0][d]), (ACS, "NT"))
                    need(d, (DVS, "TT0"))
                    Vv.tensor_tensor(w[d]["TT"], over(EYE2), w[d]["TT"], ALU.subtract).then_inc(dv_s[d], 1)
                    said_one(d)
                    mult(d, w[d]["NTl"], w[d]["NT"], over(LM[1][d]), (ACS, "NT"))
                    if lat:
                        mult(d, w[d]["Mrb"], bk(d, 2), over(INCL[d]), (PES, "Mrb"))
                    mult(d, w[d]["Lak"], bk(d, 3), over(STRICT[d]), (PES, "Lak"))
                if lat:
                    for d in range(2):
                        mult(d, w[d]["Mrk"], bk(d, 3), over(INCL[d]), (PES, "Mrk"))
                for l in levels:
                    for d in range(2):
                        if l < 5:
                            add(d, w[d]["T"], w[d]["T"], bk(d, 1), (PES, f"TX{l}"))
                        add(d, w[d]["TT"], w[d]["TT"], bk(d, 2), (PES, f"XT{l}"))
                        if l < 5:
                            mult(d, w[d]["NTl"], w[d]["NT"], over(LM[l + 1][d]))
                for d in range(2):
                    if lat:
                        add(d, pick(YY, d), pick(YY, d), bk(d, 3), (PES, "y"))
                    add(d, w[d]["ST"], w[d]["ST"], bk(d, 2), (PES, "U"))
                    mult(d, w[d]["ST"], w[d]["ST"], vec(PC[d]), (DVS, "U"))

            for sg in range(2):
                segment(sg)
                dve.wait_ge(S["mix_ready"], 4 + 6 * sg)
                if sg == 0:
                    for d in range(2):
                        Vv.memset(WORK[d]["ST"], 0.0).then_inc(S["st_zero"], 1)
                    dve.wait_ge(S["st_zero"], 2)
                else:
                    link(Vv.memset(YY[:, :, :, :], 0.0))
                dve.wait_ge(S["pj_out"], PROJ_END[sg])
                dve.wait_ge(S["kn_done"], HP * (sg + 1))
                for i in range(SC):
                    scan(sg, i)
            for d in range(2):
                dve.wait_ge(dv_s[d], DVS.before(1, SC))
            link(Vv.scalar_tensor_tensor(U1[:, :, :, :].rearrange("p c a b -> p (c a b)"),
                                         AA[0][:, :, :, :].rearrange("p c a b -> p (c a b)"), -2.0,
                                         AA[1][:, :, :, :].rearrange("p c a b -> p (c a b)"), ALU.add, ALU.add))
            for p in range(HP):
                u, k = U1[:, :, p, :], VEC["rw_k_a"] + p
                link(Vv.tensor_scalar(u, u, vecs[:, k:k + 1], 2.0, ALU.mult, ALU.add))
                link(Vv.tensor_tensor(u, u, KEY[:, :, p, :], ALU.mult))
                k = VEC["rw_r_k"] + p
                Vv.scalar_tensor_tensor(u, u, vecs[:, k:k + 1], RR[:, :, p, :], ALU.mult, ALU.mult).then_inc(S["u_ready"], 1)

            def bank3(b):
                return ps[b][:, 0:SEG].rearrange("p (c t) -> p c t", c=SC)
            for p in range(HP):
                dve.wait_ge(S["b_mm"], p + 1)
                Vv.tensor_tensor(VT[:, :, p, :], VT[:, :, p, :], bank3(p % 2), ALU.mult).then_inc(S["b_out"], 1)
            for p in range(HP):
                dve.wait_ge(S["mean_mm"], p + 1)
                Vv.scalar_tensor_tensor(YY[:, :, p, :], bank3(2 + p % 2), -1.0 / CH, YY[:, :, p, :],
                                        ALU.mult, ALU.add).then_inc(S["mean_sub"], 1)
            for p in range(HP):
                y = YY[:, :, p, :]
                dve.wait_ge(S["var_std"], p + 1)
                link(Vv.reciprocal(rstd[:, 0:SEG], std[:, 0:SEG]))
                Vv.tensor_tensor(y, y, rstd[:, 0:SEG].rearrange("p (c t) -> p c t", c=SC), ALU.mult).then_inc(S["yn"], 1)
                dve.wait_ge(S["yn"], p + 1)
                gc, bc = VEC["rw_ln_g"] + p, VEC["rw_ln_b"] + p
                link(Vv.tensor_scalar(y, y, vecs[:, gc:gc + 1], vecs[:, bc:bc + 1], ALU.mult, ALU.add))
                dve.wait_ge(S["b_out"], p + 1)
                link(Vv.tensor_tensor(y, y, VT[:, :, p, :], ALU.add))
                dve.wait_ge(S["gate_mm"], p + 1)
                Vv.tensor_tensor(y, y, bank3(6 + p % 2), ALU.mult).then_inc(S["o_in"], 1)
            post(6, O3, SEG, 1, 0, (1,))
            normalise(7, 4, X[:, :, tok_cols(1)], SEG)

            dve.wait_ge(S["logits"], 1)
            dve.wait_ge(S["consts"], 9)
            link(Vv.tensor_copy(LOG[:, :, :], ps[4][:, 0:2 * NE].rearrange("p (a b) -> p a b", a=2)))
            for t in range(2):
                mine = LOG[:, t, :].unsqueeze(2).to_broadcast([P, NE, NE])
                other = LOG[:, t, :].unsqueeze(1).to_broadcast([P, NE, NE])
                link(Vv.tensor_tensor(GT[:, t, :, :], other, mine, ALU.is_gt))
                link(Vv.tensor_tensor(EQ[:, t, :, :], other, mine, ALU.is_equal))
                link(Vv.tensor_tensor(EQ[:, t, :, :], EQ[:, t, :, :], TRI[:, :, :], ALU.mult))
                link(Vv.tensor_tensor(GT[:, t, :, :], GT[:, t, :, :], EQ[:, t, :, :], ALU.add))
                link(Vv.reduce_sum(SEL[:, t, :], GT[:, t, :, :], axis=AX.X))
                link(Vv.reduce_max(MX[:, t:t + 1], LOG[:, t, :], axis=AX.X))
            for t in range(2):
                ins = Vv.tensor_scalar(EXL[:, t, :], LOG[:, t, :], MX[:, t:t + 1], None, ALU.subtract)
            ins.then_inc(S["ex_in"], 1)
            Vv.tensor_scalar(SEL[:, :, :], SEL[:, :, :], 1.5, None, ALU.is_lt).then_inc(S["sel"], 1)
            dve.wait_ge(S["sel"], 1)
            dve.wait_ge(S["ex_out"], 1)
            link(Vv.tensor_tensor(CMB[:, :, :], SEL[:, :, :], EXL[:, :, :], ALU.mult))
            link(Vv.reduce_sum(MX[:, :], CMB[:, :, :], axis=AX.X))
            link(Vv.reciprocal(MX[:, :], MX[:, :]))
            link(Vv.tensor_tensor(CMB[:, :, :], CMB[:, :, :], MX[:, :].unsqueeze(2).to_broadcast([P, 2, NE]), ALU.mult))
            dve.wait_ge(S["pos"], 1)
            link(Vv.scalar_tensor_tensor(RK0[:, :, :], ps[5][:, 0:2 * NE].rearrange("p (a b) -> p a b", a=2), 1.0,
                                         SEL[:, :, :], ALU.add, ALU.mult))
            link(Vv.tensor_scalar(RK0[:, :, :], RK0[:, :, :], -1.0, None, ALU.add))
            link(Vv.tensor_scalar(RK1[:, :, :], RK0[:, :, :], -float(P), None, ALU.add))
            over, last, tmp = MORE[:, 0:NE], MORE[:, NE:2 * NE], MORE[:, 2 * NE:3 * NE]
            link(Vv.memset(tmp, 1.0))
            link(Vv.tensor_scalar(over, ps[5][:, 2 * NE:3 * NE], P + 0.5, None, ALU.is_gt))
            link(Vv.tensor_tensor_scan(last, tmp, over, float(NE), ALU.mult, ALU.add))
            link(Vv.tensor_copy(more_i[:, 2 * NE:2 * NE + 1], last[:, NE - 1:NE]))
            link(Vv.tensor_tensor(tmp, last, over, ALU.subtract))
            link(Vv.tensor_copy(more_i[:, 0:NE], over))
            Vv.tensor_copy(more_i[:, NE:2 * NE], tmp).then_inc(S["route"], 1)
            dve.wait_ge(S["route"], 1)

            def item(part, e, n):
                rk = (RK0, RK1)[part]
                dve.wait_ge(S["sc_out"], 4 * n)
                dve.wait_ge(S["xg"], 3 * n)
                for t in range(2):
                    pos = rk[:, t, :][:, bass.ds(e, 1)]
                    wt = CMB[:, t, :][:, bass.ds(e, 1)]
                    Vv.tensor_scalar(PG[:, t, :], SLOTS[:, :], pos, None, ALU.is_equal).then_inc(S["pg"], 1)
                    Vv.tensor_scalar(PW[:, t, :], SLOTS[:, :], pos, wt, ALU.is_equal, ALU.mult).then_inc(S["pg"], 1)
                for j in range(7):
                    dve.wait_ge(S["sil"], 7 * n + j + 1)
                    dve.wait_ge(S["moe_w"], RING + UNITS * n + 4 * j + 4)
                    if j >= 2:
                        dve.wait_ge(S["tr"], 7 * n + j - 1)
                    Vv.tensor_tensor(HH[:, j % 2, :], SX[:, j % 2, :], ps[2 * (j % 2) + 1][:, :], ALU.mult).then_inc(S["hh"], 1)
                for q in range(4):
                    dve.wait_ge(S["sc"], 4 * n + q + 1)
                    v = YA[:, 2 * q:2 * q + 2, :]
                    Vv.tensor_tensor(v, v, ps[q][:, :].rearrange("p (a b) -> p a b", a=2), ALU.add).then_inc(S["sc_out"], 1)
            with dve.Fori(0, NE) as e:
                item(0, e, e)
            second_items(dve, lambda e, n: item(1, e, n))
            post(8, YA, SEG, 1, 1, (1,))

_INS = ["x", "c", "ctx", "c_ctx", "mod_w", "mod_b", "norm_g", "gla_w_in", "gla_w_g2", "gla_b_g", "gla_norm_g",
        "gla_w_out", "rw_mu", "rw_w_rkv", "rw_w_o", "rw_w0", "rw_w1", "rw_w2", "rw_a0", "rw_a1", "rw_a2", "rw_g1",
        "rw_g2", "rw_k_k", "rw_k_a", "rw_r_k", "rw_ln_g", "rw_ln_b", "ff_w_gu", "ff_w_d", "moe_router", "moe_w_gu",
        "moe_w_d"]

def kernel(**inputs):
    import concourse.bacc as bacc
    from concourse.bass_utils import run_bass_kernel_spmd

    nc = bacc.Bacc("TRN2", target_bir_lowering=False, num_devices=1)
    arrays, aps = {}, {}
    for name in _INS:
        a = np.ascontiguousarray(inputs[name])
        arrays["in_" + name] = a
        aps[name] = nc.dram_tensor("in_" + name, a.shape, mybir.dt.from_np(a.dtype), kind="ExternalInput").ap()
    out = nc.dram_tensor("out", (1, SEG, D), F32, kind="ExternalOutput").ap()
    hybrid_backbone(nc, aps, out)
    return run_bass_kernel_spmd(nc, [arrays], core_ids=[0]).results[0]["out"]
```

```python
import concourse.bass as bass
from concourse import mybir
from contextlib import ExitStack

import numpy as np

F32 = mybir.dt.float32
ALU = mybir.AluOpType
ACT = mybir.ActivationFunctionType
AX = mybir.AxisListType

P = 128
D = 1024
KT = D // P
SEG = 256
TOK = 2 * SEG
CH = 64
NCH = TOK // CH
EPS = 1e-6

GH, GDK, GDV, GRANK = 4, 128, 256, 16
GKEY, GVAL = GH * GDK, GH * GDV
DFF = 2816
FT = DFF // P

RING = 6
SLOT = 2048

PACKS = [[("mod_b", 96), ("c", 8), ("c_ctx", 8), ("gla_b_g", 8), ("gla_norm_g", 2)],
         [("norm_g", 64), ("rw_mu", 48), ("rw_w0", 16)],
         [("rw_a0", 16), ("rw_k_k", 8), ("rw_k_a", 8), ("rw_r_k", 8), ("rw_ln_g", 8), ("rw_ln_b", 8)]]
VEC = {}
for _n, _pack in enumerate(PACKS):
    _row = 0
    for _name, _rows in _pack:
        VEC[_name] = _n * P + _row
        _row += _rows

HP = D // P
SC = SEG // CH
GW = 64
GRK = 160
DECAY = float(np.exp(-0.5))
N_MASKS = 2 * (5 + 6 * 2 * 2)
NE, FE = 8, 3584
UNITS = FE // 512 * 4 + FE // SEG
assert UNITS % RING == 0



def hybrid_backbone(nc, A, out):
    ctx = ExitStack()
    with ctx:
        def sb(name, cols):
            return ctx.enter_context(nc.sbuf_tensor(name, [P, cols], F32))

        def sem(name):
            return ctx.enter_context(nc.semaphore(name))

        X = sb("x_stream", KT * TOK)[:, :].rearrange("p (k t) -> p k t", k=KT)
        ring = sb("weight_ring", RING * SLOT)
        vecs = sb("vecs", 3 * P)
        mods = sb("mods", 2 * 96)
        totals = sb("totals", NCH)
        gain = sb("gain", 2 * 4 * 16)
        csil = sb("csil", 16)
        ident = sb("ident", P)
        ones = sb("ones", P)
        chunk_reset = sb("chunk_reset", TOK)
        masks2 = sb("masks2", 2 * P)
        mask_fwd, mask_bwd = masks2[:, 0:P], masks2[:, P:2 * P]
        sq = sb("sq", 2 * TOK)
        std = sb("std", TOK)
        rstd = sb("rstd", TOK)
        ntmp = sb("ntmp", 2 * TOK)
        ARENA = 32000
        arena = sb("arena", ARENA)
        banks = ctx.enter_context(nc.psum_tensor("banks", [P, 8 * 512], F32))
        ps = [banks[:, 512 * i:512 * i + 512] for i in range(8)]

        def at(off, *dims):
            n = 1
            for d in dims:
                n *= d
            assert off + n <= ARENA, (off, n)
            v = arena[:, off:off + n]
            if len(dims) == 2:
                return v.rearrange("p (a b) -> p a b", a=dims[0])
            if len(dims) == 3:
                return v.rearrange("p (a b c) -> p a b c", a=dims[0], b=dims[1])
            return v

        x_tm = at(0, 4, D)
        packs = at(4096, 3, P)
        H = at(0, KT, TOK)
        Y1 = at(0, KT, TOK)
        Q = at(4096, GH, TOK)
        K = at(6144, GH, TOK)
        V = at(8192, 4, GVAL)
        O1 = at(8192, KT, TOK)
        R = at(12288, KT, TOK)
        GL = at(16384, TOK)
        LA = at(16896, GH, TOK)
        E = at(18944, GH, TOK)
        QF = at(20992, GH, TOK)
        KF = at(23040, GH, TOK)
        KDT = [at(25088 + 2048 * d, 4, GKEY) for d in range(2)]
        DEC = [at(29184 + 32 * d, GH, NCH) for d in range(2)]
        W2 = at(29248, 2, GKEY)
        ATT = at(18944, 2, TOK)
        ATB = at(19968, TOK)
        ST = at(20480, 2, GDV)
        KC = at(29248, GH, TOK)
        QD, KI = [QF, Q], [KF, K]
        H2 = at(0, KT, TOK)
        HID = at(4096, FT, TOK)
        SIL = at(15360, 4, TOK)
        O2 = at(17408, KT, TOK)
        PROD = at(21504, KT, SEG)
        ACC = at(23552, 3, 2, SEG)

        KK, KEY = at(0, SC, HP, CH), at(2048, SC, HP, CH)
        AA = [at(4096 + 2048 * d, SC, HP, CH) for d in range(2)]
        SG = [at(8192 + 2048 * d, SC, HP, CH) for d in range(2)]
        VT = at(12288, SC, HP, CH)
        RR = at(14336, SC, HP, CH)
        YY = at(16384, SC, HP, CH)
        XX = at(16384, KT, SEG)
        HS = at(18432, KT, SEG)
        XJ = [at(20480 + 2048 * n, KT, SEG) for n in range(2)]
        WL, AL = at(24576, SEG), at(24832, SEG)
        LW1, LA1, LG1 = at(25088, KT, P), at(26112, KT, P), at(27136, KT, GRK)
        LW2, LA2 = at(28416, D), at(29440, D)
        G1 = at(30464, SEG)
        G2 = masks2[0:GRK - P, 0:SEG]
        LM = [[at(30720 + 64 * (2 * m + q), CH) for q in range(2)] for m in range(6)]
        STRICT = [at(30720 + 64 * (12 + q), CH) for q in range(2)]
        INCL = [at(30720 + 64 * (14 + q), CH) for q in range(2)]
        EYE2 = at(30720 + 64 * 16, CH)
        HEAD_ONES = at(31808, P)
        PC = [at(31936 + 8 * d, HP) for d in range(2)]
        KAM = at(31952, HP)
        def halves(v):
            return [v[:, 512 * n:512 * n + 512].rearrange("p (a b) -> p a b", a=HP) for n in range(2)]

        twins = [arena[:, 18432 + 1024 * n:18432 + 1024 * n + 1024] for n in range(11)]
        twins += [ring[:, 1024 * n:1024 * n + 1024] for n in range(RING * SLOT // 1024)] + [sq[:, :], ntmp[:, :]]
        WORK = []
        BLOCK_DIAGONAL = ("B", "K", "T", "NT", "A_bd", "Lak", "NTl", "TT", "X")
        for d in range(2):
            own = twins[d::2]
            WORK.append({})
            for n, name in enumerate(BLOCK_DIAGONAL):
                WORK[d][name] = own[n].rearrange("p (a b) -> p a b", a=HP)
            for n, pair in enumerate((("A", "R"), ("Vt", "Mrb"), ("Mrk", "W"))):
                WORK[d].update(zip(pair, halves(own[9 + n])))
            last = halves(own[12]) if d == 0 else [v[:, :].rearrange("p (a b) -> p a b", a=HP) for v in (std, rstd)]
            WORK[d].update(zip(("SA", "sum"), last))
            WORK[d]["e2"] = WORK[d]["sum"]
            WORK[d]["e1"] = WORK[d]["A"]
            WORK[d]["e3"] = X[:, :, CH * (2 + d):CH * (2 + d) + CH]
            WORK[d]["t"], WORK[d]["kka"] = halves(own[7])
            WORK[d]["V"] = WORK[d]["T"]
            WORK[d]["ST"] = X[:, :, CH * d:CH * d + CH]
        U1 = at(4096, SC, HP, CH)
        GW2A, GW2B = at(18432, D), at(19456, D)
        O3 = at(20480, KT, SEG)
        H3 = at(0, KT, SEG)
        HTM = at(2048, 2, D)
        XG = at(4096, KT, P)
        HX = at(5120, FE // P, P)
        SX = at(8704, 2, 512)
        HH = at(9728, 2, 512)
        YS = at(10752, D)
        PG = at(11776, 2, P)
        PW = at(12032, 2, P)
        PWT = at(12288, SEG)
        YA = at(12544, KT, SEG)
        RT = at(14592, KT, NE)
        LOG = at(14656, 2, NE)
        SEL, CMB, RK0, RK1, EXL = (at(14672 + 16 * n, 2, NE) for n in range(5))
        GT, EQ = at(14752, 2, NE, NE), at(14880, 2, NE, NE)
        TRI = at(15008, NE, NE)
        SLOTS = at(15072, P)
        BEFORE = at(15200, P)
        MX = at(15328, 2)
        MORE = at(15330, 3 * NE)
        OT = at(15360, 2, D)
        more_i = at(17408, 2 * NE + 1).bitcast(mybir.dt.int32)

        S = {n: sem(n) for n in (
            "x_in vec_in small_in consts zeroed "
            "ff_mm x_t x_t_out vec_t vec_out csil mod_mm mod_acc mod_part mod_out "
            "sq_ready sq_used std_ready nt_ready h_ready post_done "
            "pj pj_out gla_prep_v gla_prep_s kd_t kd_t_out "
            "att att_out att_m sup snew sinter y_out fn_sq fn_ss fn_std fn_done "
            "ff_sil ff_hid ffd ffd_out "
            "rw_small mix_ready k_sq kn_mm kn_max kn_sqrt kn_rcp kn_done masks1 "
            "st_zero off_zero u_ready b_mm b_out mean_mm mean_sub var_sq var_mm var_std yn gate_mm o_in "
            "h_tm h_tm_out rt_in logits ex_in ex_out sel pos route pg xg xg_out sil hh tr tr_out yd_out sc sc_out moe_w "
            "v_chain s_chain p_chain out_t out_c stored").split()}
        def mod(layer, j, k, sg):
            c = 96 * layer + 2 * (8 * j + k) + (1 - sg)
            return mods[:, c:c + 1]

        def pre_gain(layer, sub, k, sg):
            c = (layer * 4 + 2 * sub) * 16 + 2 * k + (1 - sg)
            return gain[:, c:c + 1]

        def post_gain(layer, sub, k, sg):
            c = (layer * 4 + 2 * sub + 1) * 16 + 2 * k + (1 - sg)
            return gain[:, c:c + 1]

        def second_items(eng, item):
            eng.wait_ge(S["route"], 1)
            with eng.Fori(0, NE) as e:
                over = eng.value_load(more_i[0:1, bass.ds(e, 1)], min_val=0, max_val=1)
                n = eng.value_load(more_i[0:1, bass.ds(e + NE, 1)], min_val=NE, max_val=2 * NE)
                with eng.If(over > 0):
                    item(e, n)
            return eng.value_load(more_i[0:1, 2 * NE:2 * NE + 1], min_val=NE, max_val=2 * NE)

        def two_banks(b):
            return banks[:, 512 * b:512 * b + 1024].rearrange("p (a b) -> p a b", a=HP)

        def by_chunk(bank):
            return bank[:, 0:SEG].rearrange("p (c t) -> p c t", c=SC)

        def tok_cols(sg):
            return slice(SEG * sg, SEG * sg + SEG)

        pe_s = [sem(f"scan_pe{d}") for d in range(2)]
        dv_s = [sem(f"scan_dve{d}") for d in range(2)]
        ac_s = [sem(f"scan_act{d}") for d in range(2)]
        pre_v = [sem(f"pre_dve{d}") for d in range(2)]
        pre_s = [sem(f"pre_act{d}") for d in range(2)]
        w_in = [sem(f"w_in{i}") for i in range(RING)]
        N_SMALL = 2

        def cols256(w, n, width=256):
            v = w.rearrange("(k p) n -> p k n", p=P)
            return [v[:, :, i * 256:i * 256 + width] for i in range(n)]
        chunks, frees, first = [], [], {}

        def stream(name, views, said, start, step):
            first[name] = len(chunks)
            for i, v in enumerate(views):
                chunks.append(v)
                frees.append((S[said], start + step * (i + 1)))
        stream("mod0", cols256(A["mod_w"][0], 24), "mod_mm", 0, 1)
        w_in_gla = A["gla_w_in"][0]
        stream("gla_k", cols256(w_in_gla[:, GKEY:2 * GKEY], 2), "pj", 0, 2)
        stream("gla_q", cols256(w_in_gla[:, 0:GKEY], 2), "pj", 4, 2)
        stream("gla_g", [w_in_gla.rearrange("(k p) n -> p k n", p=P)[:, :, 3072:3104]], "pj", 8, 1)
        stream("gla_v", cols256(w_in_gla[:, 1024:2048], 4), "pj", 13, 4)
        stream("gla_r", cols256(w_in_gla[:, 2048:3072], 4), "pj", 33, 2)
        stream("gla_o", cols256(A["gla_w_out"][0], 4), "pj", 41, 2)
        ffa, ffb = cols256(A["ff_w_gu"][0][:, 0:DFF], 11), cols256(A["ff_w_gu"][0][:, DFF:2 * DFF], 11)
        mod1 = cols256(A["mod_w"][1], 24)
        n_pairs = FT // 2
        mod_chunks = [range(24 * p // (n_pairs - 1), 24 * (p + 1) // (n_pairs - 1)) for p in range(n_pairs - 1)] + [range(0)]
        for p in range(n_pairs):
            stream(f"mod1_{p}", [mod1[i] for i in mod_chunks[p]], "mod_acc", 24 * p // (n_pairs - 1), 1)
            stream(f"ff_gu{p}", [ffa[p], ffb[p]], "ff_mm", 4 * p, 2)
        stream("ff_d", [A["ff_w_d"][0].rearrange("(k p) n -> p k n", p=P)[:, 2 * i:2 * i + 2, :] for i in range(11)], "ffd", 0, 1)
        rkv = A["rw_w_rkv"][0]
        PJ1 = [49, 49 + 50]
        PROJ_END = [49 + 50, 49 + 50 + 60]
        KEY_PJ = [p + 34 for p in PJ1]
        MIX_DONE = [PJ1[sg] + n for sg, ns in enumerate(((1, 18, 42, 50), (1, 18, 42, 50, 58, 60))) for n in ns]
        for sg in range(2):
            for n, name in ((1, "k"), (2, "v"), (0, "r"))[:2 + sg]:
                stream(f"rw_{name}{sg}", cols256(rkv[n], 4), "pj", PJ1[sg] + 34 + 8 * "kvr".index(name), 2)
        stream("rw_o", cols256(A["rw_w_o"][0], 4), "pj", PROJ_END[1], 2)
        cid_moe = len(chunks)

        levels = range(1, 6)
        PE_STEPS, DV_STEPS, AC_STEPS = [], [], []
        for lat in range(2):
            PE_STEPS.append(["NT"] + ["Mrb"] * lat + ["Lak"] + ["Mrk"] * lat + ["Vt", "Bt", "T0", "Kt"]
                            + [x for l in levels for x in [f"X{l}"] + [f"TT{l - 1}"] * (l > 1) + [f"TX{l}"]]
                            + ["W", "TT5", "SA"] + ["y"] * lat + ["U"])
            DV_STEPS.append(["kka", "B0", "B"] + ["R"] * lat + ["PC", "t1", "t2", "t3", "K0", "K", "TT0", "TT"]
                            + ["NTl1"] + ["Mrb"] * lat + ["Lak0", "Lak"] + ["Mrk"] * lat
                            + [x for l in levels for x in [f"NTl{l + 1}"] * (l < 5) + [f"T{l}"]]
                            + ["y"] * lat + ["U", "ST"])
            AC_STEPS.append(["V0", "V", "NT0", "NT", "A0", "A_bd", "Vt0", "Vt", "Bt", "T0", "Kt"]
                            + [x for l in levels for x in [f"X{l}"] + [f"TT{l - 1}"] * (l > 1)] + ["W", "TT5", "SA"])

        class Steps:

            def __init__(self, steps, sems):
                self.steps, self.sems = steps, sems

            def value(self, lat, i, name):
                n = len(self.steps[lat])
                return SC * len(self.steps[0]) * lat + i * n + self.steps[lat].index(name) + 1

            def before(self, lat, i):
                return SC * len(self.steps[0]) * lat + i * len(self.steps[lat])
        PES, DVS, ACS = Steps(PE_STEPS, pe_s), Steps(DV_STEPS, dv_s), Steps(AC_STEPS, ac_s)
        all_scanned = SC * (len(PE_STEPS[0]) + len(PE_STEPS[1]))

        def slot(cid, k):
            v = ring[:, (cid % RING) * SLOT:(cid % RING + 1) * SLOT]
            return v.rearrange("p (k n) -> p k n", k=k)

        def arrived(eng, cid):
            eng.wait_ge(w_in[cid % RING], 16 * (cid // RING + 1))

        block = ctx.enter_context(nc.Block())

        @block.sync
        def _(sp):
            for n, name in enumerate(("ctx", "x")):
                sp.dma_start(x_tm[:, 2 * n:2 * n + 2, :],
                             A[name][0].rearrange("(t p) d -> p t d", p=P)).then_inc(S["x_in"], 16)
            for n, pack in enumerate(PACKS):
                row = 0
                for name, rows in pack:
                    v = A[name]
                    while len(v.shape) > 2:
                        v = v.rearrange("a b ... -> (a b) ...")
                    if len(v.shape) == 2:
                        v = v.rearrange("a b -> (a b)")
                    sp.dma_start(packs[row:row + rows, n, :], v.rearrange("(r c) -> r c", c=P)).then_inc(S["vec_in"], 16)
                    row += rows
            for cid, src in enumerate(chunks):
                if cid >= RING:
                    sp.wait_ge(*frees[cid - RING])
                for lat, name in enumerate(("rw_k1", "rw_o")):
                    if cid == first[name]:
                        for d in range(2):
                            sp.wait_ge(dv_s[d], DVS.before(lat, SC))
                kk, cc = src.shape[1], src.shape[2]
                dst = ring[:, (cid % RING) * SLOT:(cid % RING) * SLOT + kk * cc].rearrange("p (k n) -> p k n", k=kk)
                sp.dma_start(dst, src).then_inc(w_in[cid % RING], 16)
                if cid == RING - 1:
                    sp.wait_ge(S["vec_out"], 3)
                    sp.wait_ge(S["x_t_out"], KT)
                    sp.wait_ge(S["zeroed"], 1)
                    for d in range(2):
                        sp.dma_start(W2[16 * d:16 * d + 16, d, :], A["gla_w_g2"][0, d]).then_inc(S["small_in"], 16)
            gu, wd = A["moe_w_gu"][0], A["moe_w_d"][0]

            def expert(e, n):
                u = 0
                for j in range(FE // 512):
                    for half in range(2):
                        for kh in range(2):
                            col = half * FE + 512 * j
                            src = gu[e, :, col:col + 512].rearrange("(k p) n -> p k n", p=P)[:, 4 * kh:4 * kh + 4, :]
                            sp.wait_ge(S["moe_w"], UNITS * n + u + 1)
                            sp.dma_start(slot(cid_moe + u, 4), src).then_inc(w_in[(cid_moe + u) % RING], 16)
                            u += 1
                for i in range(FE // SEG):
                    src = wd[e, SEG * i:SEG * i + SEG, :].rearrange("(k p) n -> p k n", p=P)
                    sp.wait_ge(S["moe_w"], UNITS * n + u + 1)
                    sp.dma_start(slot(cid_moe + u, 2), src).then_inc(w_in[(cid_moe + u) % RING], 16)
                    u += 1
            with sp.Fori(0, NE) as e:
                expert(e, e)
            second_items(sp, expert)
            sp.wait_ge(S["out_c"], 4)
            sp.dma_start(out[0].rearrange("(t p) d -> p t d", p=P), OT[:, :, :]).then_inc(S["stored"], 16)
            sp.wait_ge(S["stored"], 16)

        @block.gpsimd
        def _(pool):
            g = nc.gpsimd
            n = [0]

            def link(ins):
                n[0] += 1
                ins.then_inc(S["p_chain"], 1)
                pool.wait_ge(S["p_chain"], n[0])
            link(g.memset(ident[:, :], 0.0))
            g.affine_select(out=ident[:, :], in_=ident[:, :], compare_op=ALU.not_equal, fill=1.0, base=0,
                            pattern=[[-1, P]], channel_multiplier=1).then_inc(S["consts"], 1)
            g.memset(ones[:, :], 1.0).then_inc(S["consts"], 1)
            link(g.memset(chunk_reset[:, :], 1.0))
            g.memset(chunk_reset[:, ::CH], 0.0).then_inc(S["consts"], 1)
            link(g.memset(mask_fwd[:, :], 1.0))
            link(g.memset(mask_bwd[:, :], 1.0))
            link(g.memset(mask_fwd[CH:P, 0:CH], 0.0))
            link(g.memset(mask_bwd[0:CH, CH:P], 0.0))
            g.affine_select(out=mask_fwd[:, :], in_=mask_fwd[:, :], compare_op=ALU.is_ge, fill=0.0, base=0,
                            pattern=[[1, P]], channel_multiplier=-1).then_inc(S["consts"], 1)
            g.affine_select(out=mask_bwd[:, :], in_=mask_bwd[:, :], compare_op=ALU.is_ge, fill=0.0, base=0,
                            pattern=[[-1, P]], channel_multiplier=1).then_inc(S["consts"], 1)
            pool.wait_ge(S["consts"], 5)
            link(g.memset(mask_fwd[0:CH, CH:P], 0.0))
            g.memset(mask_bwd[CH:P, 0:CH], 0.0).then_inc(S["consts"], 1)
            pool.wait_ge(S["x_t"], KT)
            pool.wait_ge(S["vec_t"], 3)
            g.memset(W2[0:32, :, :], 0.0).then_inc(S["zeroed"], 1)

            pool.wait_ge(S["post_done"], KT)
            for q in range(2):
                rows = slice(CH * q, CH * q + CH)

                def select(v, op, base, mult, pattern):
                    g.affine_select(out=v[rows], in_=v[rows], compare_op=op, fill=0.0, base=base,
                                    pattern=pattern, channel_multiplier=mult).then_inc(S["masks1"], 1)
                    count[0] += 1
                    pool.wait_ge(S["masks1"], count[0])
                if q == 0:
                    count = [0]
                    for v in [x for m in LM for x in m] + STRICT + INCL + [EYE2]:
                        link(g.memset(v, 1.0))
                    link(g.memset(HEAD_ONES[:, :], 0.0))
                    link(g.memset(HEAD_ONES[0:CH, 0:CH], 1.0))
                    link(g.memset(HEAD_ONES[CH:P, CH:P], 1.0))
                select(STRICT[0], ALU.is_gt, 0, -1, [[1, CH]])
                select(STRICT[1], ALU.is_gt, 0, 1, [[-1, CH]])
                select(INCL[0], ALU.is_ge, 0, -1, [[1, CH]])
                select(INCL[1], ALU.is_ge, 0, 1, [[-1, CH]])
                select(EYE2, ALU.is_equal, 0, 1, [[-1, CH]])
                for m in range(6):
                    h, b, nb = 2 ** m, 2 ** (m + 1), CH // 2 ** (m + 1)
                    for w in range(2):
                        cols = LM[m][w].rearrange("p (n z) -> p n z", z=b)
                        link(g.memset(cols[rows, :, (0 if w == 0 else h):(h if w == 0 else b)], 0.0))
                        lo = h if w == 1 else 0
                        select(cols, ALU.is_ge, -lo, 1, [[-b, nb], [0, b]])
                        select(cols, ALU.is_ge, lo + h - 1, -1, [[b, nb], [0, b]])
            assert count[0] == N_MASKS
            for sg in range(2):
                if sg == 1:
                    for d in range(2):
                        pool.wait_ge(pe_s[d], PES.before(0, SC))
                        pool.wait_ge(dv_s[d], DVS.before(0, SC))
                for dst, src in ([(LW1[:, :, CH * d:CH * d + CH], A["rw_w1"][0, d].rearrange("(k p) n -> p k n", p=P)) for d in range(2)]
                                 + [(LA1[:, :, CH * d:CH * d + CH], A["rw_a1"][0, d].rearrange("(k p) n -> p k n", p=P)) for d in range(2)]
                                 + [(LG1[:, :, :], A["rw_g1"][0].rearrange("(k p) n -> p k n", p=P)),
                                    (LW2[:, :], A["rw_w2"][0].rearrange("a b n -> (a b) n")),
                                    (LA2[:, :], A["rw_a2"][0].rearrange("a b n -> (a b) n"))]):
                    pool.dma_start(dst, src).then_inc(S["rw_small"], 16)
                pool.wait_ge(S["pj_out"], PROJ_END[sg])
                pool.wait_ge(S["mix_ready"], 4 + 6 * sg)
                pool.wait_ge(S["kn_done"], HP * (sg + 1))
                for name in BLOCK_DIAGONAL[:6]:
                    for d in range(2):
                        g.memset(WORK[d][name], 0.0).then_inc(S["off_zero"], 1)
            for d in range(2):
                pool.wait_ge(pe_s[d], all_scanned)
                pool.wait_ge(dv_s[d], DVS.before(1, SC))
            pool.dma_start(GW2A[:, :], A["rw_g2"][0, 0:P, :]).then_inc(S["rw_small"], 16)
            pool.dma_start(GW2B[0:GRK - P, :], A["rw_g2"][0, P:GRK, :]).then_inc(S["rw_small"], 16)
            pool.wait_ge(S["post_done"], 3 * KT)
            pool.dma_start(RT[:, :, :], A["moe_router"][0].rearrange("(k p) n -> p k n", p=P)).then_inc(S["rt_in"], 16)
            link(g.memset(TRI[:, :, :], 1.0))
            link(g.memset(BEFORE[:, :], 1.0))
            link(g.memset(YA[:, :, :], 0.0))
            g.affine_select(out=TRI[:, :, :], in_=TRI[:, :, :], compare_op=ALU.is_gt, fill=0.0, base=0,
                            pattern=[[1, NE], [-1, NE]], channel_multiplier=0).then_inc(S["consts"], 1)
            g.affine_select(out=BEFORE[:, :], in_=BEFORE[:, :], compare_op=ALU.is_gt, fill=0.0, base=0,
                            pattern=[[1, P]], channel_multiplier=-1).then_inc(S["consts"], 1)
            g.iota(SLOTS[:, :], pattern=[[1, P]], base=0, channel_multiplier=0, allow_small_or_imprecise_dtypes=True).then_inc(S["consts"], 1)

        @block.tensor
        def _(pe):
            T = nc.tensor

            def norm_stats(n, width):
                for k in range(KT):
                    pe.wait_ge(S["sq_ready"], KT * n + k + 1)
                    T.matmul(ps[7][:, 0:width], ones[:, :], sq[:, (k % 2) * TOK:(k % 2) * TOK + width],
                             start=(k == 0), stop=(k == KT - 1)).then_inc(S["sq_used"], 1)

            pe.wait_ge(S["consts"], 6)
            pe.wait_ge(S["vec_in"], 16 * sum(len(p) for p in PACKS))
            for n, pack in enumerate(PACKS):
                rows = sum(r for _, r in pack)
                T.transpose(ps[6][:, n * P:n * P + rows], packs[0:rows, n, :], ident[0:rows, 0:rows]).then_inc(S["vec_t"], 1)
            pe.wait_ge(S["x_in"], 32)
            for k in range(KT):
                if k >= 6:
                    pe.wait_ge(S["x_t_out"], k - 5)
                for t in range(4):
                    ins = T.transpose(ps[k % 6][:, t * P:t * P + P], x_tm[:, t, k * P:k * P + P], ident[:, :])
                ins.then_inc(S["x_t"], 1)

            def modulation():
                bank = ps[6]
                for i in range(24):
                    arrived(pe, first["mod0"] + i)
                    w = slot(first["mod0"] + i, KT)
                    for j in range(2):
                        o = bank[:, 4 * i + 2 * j:4 * i + 2 * j + 2]
                        for k in range(KT):
                            ins = T.matmul(o, w[:, k, j * P:j * P + P], csil[:, 2 * k:2 * k + 2],
                                           start=(k == 0), stop=(k == KT - 1))
                    ins.then_inc(S["mod_mm"], 1)

            pe.wait_ge(S["csil"], 2)
            modulation()
            norm_stats(0, TOK)

            tile = [0]

            def next_bank():
                n = tile[0]
                tile[0] += 1
                if n >= 6:
                    pe.wait_ge(S["pj_out"], n - 5)
                return ps[n % 6]

            def project(cid, src, width, n_chunks):
                for i in range(n_chunks):
                    arrived(pe, cid + i)
                    w = slot(cid + i, KT)
                    for j in range(2):
                        b = next_bank()
                        for k in range(KT):
                            ins = T.matmul(b[:, 0:width], w[:, k, j * P:j * P + P], src[:, k, :],
                                           start=(k == 0), stop=(k == KT - 1))
                        ins.then_inc(S["pj"], 1)

            for k in range(KT):
                pe.wait_ge(S["h_ready"], k + 1)
            project(first["gla_k"], H, TOK, 2)
            project(first["gla_q"], H, TOK, 2)
            cid = first["gla_g"]
            arrived(pe, cid)
            w = ring[:, (cid % RING) * SLOT:(cid % RING) * SLOT + 32 * KT].rearrange("p (k n) -> p k n", k=KT)
            b = next_bank()
            for k in range(KT):
                ins = T.matmul(b[0:32, :], w[:, k, :], H[:, k, :], start=(k == 0), stop=(k == KT - 1))
            ins.then_inc(S["pj"], 1)
            pe.wait_ge(S["pj_out"], 9)
            pe.wait_ge(S["small_in"], 32)

            def gate_tiles(d):
                for h in range(GH):
                    T.matmul(next_bank()[:, :], W2[0:32, d, h * P:h * P + P], GL[0:32, :],
                             start=True, stop=True).then_inc(S["pj"], 1)

            def keys_by_token(d):
                pe.wait_ge(S["gla_prep_v"], 5 * d + 5)
                for t in range(4):
                    n = 4 * d + t
                    if n >= 2:
                        pe.wait_ge(S["kd_t_out"], n - 1)
                    for h in range(GH):
                        ins = T.transpose(ps[6 + n % 2][:, h * P:h * P + P], E[:, h, t * P:t * P + P], ident[:, :])
                    ins.then_inc(S["kd_t"], 1)

            gate_tiles(0)
            for i in range(4):
                cid = first["gla_v"] + i
                arrived(pe, cid)
                w = slot(cid, KT)
                for t in range(4):
                    b = next_bank()
                    for k in range(KT):
                        ins = T.matmul(b[:, 0:256], H[:, k, t * P:t * P + P], w[:, k, :],
                                       start=(k == 0), stop=(k == KT - 1))
                    ins.then_inc(S["pj"], 1)
            keys_by_token(0)
            gate_tiles(1)
            project(first["gla_r"], H, TOK, 4)
            keys_by_token(1)
            pe.wait_ge(S["pj_out"], tile[0])
            pe.wait_ge(S["kd_t_out"], 8)

            for h in range(GH):
                if h >= 1:
                    pe.wait_ge(S["att_out"], 2 * h)
                for d in range(2):
                    for t in range(4):
                        ins = T.matmul(ps[d][:, t * P:t * P + P], KI[d][:, h, t * P:t * P + P],
                                       QD[d][:, h, t * P:t * P + P], start=True, stop=True)
                    ins.then_inc(S["att"], 1)
                pe.wait_ge(S["att_m"], h + 1)
                if h >= 1:
                    pe.wait_ge(S["y_out"], 2 * h)
                for vt in range(2):
                    for t in range(4):
                        T.matmul(ps[2 + vt][:, t * P:t * P + P], V[:, t, h * GDV + vt * P:h * GDV + vt * P + P],
                                 ATT[:, h % 2, t * P:t * P + P], start=(t == 0), stop=False, skip_group_check=True)
                for i in range(NCH):
                    for d in range(2):
                        if i < NCH - 1:
                            n = (NCH - 1) * h + i
                            if n >= 2:
                                pe.wait_ge(S["snew"], 2 * (n - 2) + d + 1)
                            c = i if d == 0 else (3 - i if i < 4 else 11 - i)
                            r0 = CH * (c % 2)
                            T.matmul(ps[4 + d + 2 * (n % 2)][:, 0:GDV],
                                     KDT[d][r0:r0 + CH, c // 2, h * P:h * P + P],
                                     V[r0:r0 + CH, c // 2, h * GDV:h * GDV + GDV],
                                     start=True, stop=True).then_inc(S["sup"], 1)
                    if i >= 1:
                        for d in range(2):
                            n = (NCH - 1) * h + i
                            c = i if d == 0 else (3 - i if i < 4 else 11 - i)
                            pe.wait_ge(S["snew"], 2 * (n - 1) + d + 1)
                            for vt in range(2):
                                ins = T.matmul(ps[2 + vt][:, c * CH:c * CH + CH], ST[:, d, vt * P:vt * P + P],
                                               QD[d][:, h, c * CH:c * CH + CH], start=False,
                                               stop=(i == NCH - 1 and d == 1), skip_group_check=True)
                            ins.then_inc(S["sinter"], 1)

            for h in range(GH):
                for vt in range(2):
                    pe.wait_ge(S["fn_sq"], 2 * h + vt + 1)
                    T.matmul(ps[h % 2][:, :], ones[:, :], sq[:, vt * TOK:vt * TOK + TOK],
                             start=(vt == 0), stop=(vt == 1)).then_inc(S["fn_ss"], 1)
            pe.wait_ge(S["fn_done"], KT)
            project(first["gla_o"], Y1, TOK, 4)
            norm_stats(1, TOK)
            norm_stats(2, TOK)

            for k in range(KT):
                pe.wait_ge(S["h_ready"], KT + k + 1)
            for p in range(FT // 2):
                for ab in range(2):
                    if ab == 0:
                        if p >= 2:
                            pe.wait_ge(S["ff_hid"], 2 * (p - 1))
                        if p >= 1:
                            pe.wait_ge(S["mod_acc"], mod_chunks[p - 1][-1] + 1)
                            for i in range(len(mod_chunks[p - 1])):
                                for t in range(2):
                                    for sg in range(2):
                                        c = 4 * i + 2 * t + sg
                                        ins = T.matmul(ps[4 * (p % 2) + 3][:, c:c + 1], ACC[:, i, sg, t * P:t * P + P],
                                                       ones[:, 0:1], start=True, stop=True)
                            ins.then_inc(S["mod_mm"], 1)
                    cid = first[f"ff_gu{p}"] + ab
                    arrived(pe, cid)
                    w = slot(cid, KT)
                    for j in range(2):
                        if ab == 1 and j == 1 and p >= 1:
                            pe.wait_ge(S["mod_part"], p)
                        for k in range(KT):
                            ins = T.matmul(ps[4 * (p % 2) + 2 * ab + j][:, :], w[:, k, j * P:j * P + P], H2[:, k, :],
                                           start=(k == 0), stop=(k == KT - 1))
                        ins.then_inc(S["ff_mm"], 1)
            pe.wait_ge(S["ff_hid"], FT)
            cid = first["ff_d"]
            for i in range(FT // 2):
                arrived(pe, cid + i)
                w = slot(cid + i, 2)
                for j in range(KT):
                    for k in range(2):
                        ins = T.matmul(ps[j][:, :], w[:, k, j * P:j * P + P], HID[:, 2 * i + k, :],
                                       start=(i == 0 and k == 0), stop=(i == FT // 2 - 1 and k == 1))
                ins.then_inc(S["ffd"], 1)
            pe.wait_ge(S["ffd_out"], KT)
            norm_stats(3, TOK)

            pe.wait_ge(S["masks1"], N_MASKS)
            jn = [0]

            def mix(sg):
                pe.wait_ge(S["mix_ready"], jn[0] + 1)
                jn[0] += 1
                return XJ[(jn[0] - 1) % 2]

            def hidden(w, cols, src):
                b = next_bank()
                for k in range(KT):
                    ins = T.matmul(b[0:cols, 0:SEG], w[:, k, :], src[:, k, :], start=(k == 0), stop=(k == KT - 1))
                ins.then_inc(S["pj"], 1)

            def segment(sg):
                norm_stats(4 + sg, SEG)
                pe.wait_ge(S["rw_small"], 16 * 7 * (sg + 1))
                for w1, w2, hid in ((LW1, LW2, WL), (LA1, LA2, AL)):
                    hidden(w1, P, mix(sg))
                    pe.wait_ge(S["pj_out"], tile[0])
                    for d in range(2):
                        for p in range(HP):
                            T.matmul(next_bank()[:, 0:SEG], w2[CH * d:CH * d + CH, p * P:p * P + P],
                                     hid[CH * d:CH * d + CH, :], start=True, stop=True).then_inc(S["pj"], 1)
                project(first[f"rw_k{sg}"], mix(sg), SEG, 4)
                for p in range(HP):
                    pe.wait_ge(S["k_sq"], HP * sg + p + 1)
                    if p >= 2 or sg:
                        pe.wait_ge(S["kn_max"], HP * sg + p - 1)
                    T.matmul(ps[6 + p % 2][:, 0:SEG], HEAD_ONES[:, :], sq[:, (p % 2) * TOK:(p % 2) * TOK + SEG],
                             start=True, stop=True).then_inc(S["kn_mm"], 1)
                project(first[f"rw_v{sg}"], mix(sg), SEG, 4)
                if sg:
                    project(first["rw_r1"], mix(sg), SEG, 4)
                    src = mix(sg)
                    hidden(LG1[:, :, 0:P], P, src)
                    hidden(LG1[:, :, P:GRK], GRK - P, src)
                pe.wait_ge(S["pj_out"], tile[0])
                pe.wait_ge(S["kn_done"], HP * (sg + 1))

            def scan(lat, i):
                bank = [ps[4 * d:4 * d + 4] for d in range(2)]
                rows = [slice(0, CH), slice(CH, P)]

                def heads(d, name, b, terms, need):
                    for c, n in need:
                        pe.wait_ge(c.sems[d], c.value(lat, i, n))
                    for p in range(HP):
                        for q, (lhs, rhs) in enumerate(terms):
                            for r in rows:
                                ins = T.matmul(bank[d][b][r, p * CH:p * CH + CH], lhs[r, p, :], rhs[r, p, :],
                                               start=(q == 0), stop=(q == len(terms) - 1))
                    ins.then_inc(pe_s[d], 1)

                def pairs(d, name, out, terms, need):
                    for c, n in need:
                        pe.wait_ge(c.sems[d], c.value(lat, i, n))
                    for p in range(HP):
                        for q, (lhs, rhs) in enumerate(terms):
                            if rhs is None:
                                ins = T.transpose(out[:, p, :], lhs[:, p, :], ident[:, :])
                            else:
                                ins = T.matmul(out[:, p, :], lhs[:, p, :], rhs[:, p, :],
                                               start=(q == 0), stop=(q == len(terms) - 1))
                    ins.then_inc(pe_s[d], 1)

                def bk(d, b):
                    return bank[d][b].rearrange("p (a b) -> p a b", a=HP)

                def bk2(d, b):
                    return two_banks(4 * d + b)
                both = range(2)
                w = WORK
                for d in both:
                    pairs(d, "NT", bk(d, 0), [(w[d]["B"], w[d]["A"])], [(DVS, "B")])
                    if lat:
                        pairs(d, "Mrb", bk(d, 1), [(w[d]["B"], w[d]["R"])], [(DVS, "R")])
                for d in both:
                    pairs(d, "Lak", bk(d, 2), [(w[d]["K"], w[d]["A"])], [(DVS, "K")])
                    if lat:
                        pairs(d, "Mrk", bk(d, 3), [(w[d]["K"], w[d]["R"])], [])
                for d in both:
                    pairs(d, "Vt", bk2(d, 0), [(w[d]["V"], None)], [(ACS, "NT")] + [(DVS, "Mrb")] * lat)
                for d in both:
                    pairs(d, "Bt", bk2(d, 2), [(w[d]["B"], None)], [(DVS, "Mrk" if lat else "Lak")])
                for d in both:
                    pairs(d, "T0", bk2(d, 0), [(w[d]["TT"], None)], [(DVS, "TT"), (ACS, "Vt")])
                for d in both:
                    pairs(d, "Kt", bk2(d, 2), [(w[d]["K"], None)], [(ACS, "Bt")])
                for l in levels:
                    for d in both:
                        if l == 1:
                            pairs(d, "X", bk2(d, 0), [(w[d]["NTl"], w[d]["T"])], [(DVS, "NTl1"), (ACS, "T0")])
                        else:
                            pairs(d, "X", bk2(d, 0), [(w[d]["NTl"], w[d]["T"])], [(DVS, f"T{l - 1}"), (ACS, f"X{l - 1}")])
                            pairs(d, "TT", bk2(d, 2), [(w[d]["T"], None)], [])
                    for d in both:
                        pairs(d, "TX", bk2(d, 2), [(w[d]["TT"], w[d]["X"])], [(ACS, f"X{l}" if l == 1 else f"TT{l - 1}")])
                for d in both:
                    pe.wait_ge(dv_s[d], DVS.before(lat, i))
                    pairs(d, "W", bk(d, 0), [(w[d]["A_bd"], w[d]["ST"]), (w[d]["Lak"], w[d]["Vt"])], [(ACS, "X5")])
                for d in both:
                    pairs(d, "TT", bk2(d, 2), [(w[d]["T"], None)], [(DVS, "T5")])
                for d in both:
                    pairs(d, "SA", bk(d, 1), [(w[d]["TT"], w[d]["W"])], [(ACS, "TT5")])
                for d in both:
                    t_y = [(w[d]["ST"], w[d]["R"]), (w[d]["SA"], w[d]["Mrb"]), (w[d]["Vt"], w[d]["Mrk"])]
                    if lat:
                        heads(d, "y", 3, t_y, [(ACS, "SA")])
                    pairs(d, "U", bk(d, 2), [(w[d]["B"], w[d]["SA"]), (w[d]["K"], w[d]["Vt"])], [(ACS, "SA")])

            for sg in range(2):
                segment(sg)
                if sg == 0:
                    pe.wait_ge(S["st_zero"], 2)
                for i in range(SC):
                    scan(sg, i)
            for d in range(2):
                pe.wait_ge(dv_s[d], DVS.before(1, SC))
            for p in range(HP):
                pe.wait_ge(S["u_ready"], p + 1)
                if p >= 2:
                    pe.wait_ge(S["b_out"], p - 1)
                T.matmul(by_chunk(ps[p % 2]), HEAD_ONES[:, :], U1[:, :, p, :], start=True, stop=True).then_inc(S["b_mm"], 1)
            for p in range(HP):
                if p >= 2:
                    pe.wait_ge(S["mean_sub"], p - 1)
                T.matmul(by_chunk(ps[2 + p % 2]), HEAD_ONES[:, :], YY[:, :, p, :], start=True, stop=True).then_inc(S["mean_mm"], 1)
            pe.wait_ge(S["rw_small"], 16 * 16)
            for p in range(HP):
                pe.wait_ge(S["var_sq"], p + 1)
                if p >= 2:
                    pe.wait_ge(S["var_std"], p - 1)
                T.matmul(ps[4 + p % 2][:, 0:SEG], HEAD_ONES[:, :], sq[:, (p % 2) * TOK:(p % 2) * TOK + SEG],
                         start=True, stop=True).then_inc(S["var_mm"], 1)
                if p >= 2:
                    pe.wait_ge(S["o_in"], p - 1)
                T.matmul(ps[6 + p % 2][:, 0:SEG], GW2A[:, p * P:p * P + P], G1[:, :], start=True, stop=False)
                T.matmul(ps[6 + p % 2][:, 0:SEG], GW2B[0:GRK - P, p * P:p * P + P], G2, start=False,
                         stop=True).then_inc(S["gate_mm"], 1)
            pe.wait_ge(S["o_in"], HP)

            for i in range(4):
                arrived(pe, first["rw_o"] + i)
                w = slot(first["rw_o"] + i, KT)
                for j in range(2):
                    b = next_bank()
                    for k in range(KT):
                        ins = T.matmul(by_chunk(b), w[:, k, j * P:j * P + P], YY[:, :, k, :],
                                       start=(k == 0), stop=(k == KT - 1))
                    ins.then_inc(S["pj"], 1)
            pe.wait_ge(S["pj_out"], tile[0])
            norm_stats(6, SEG)
            norm_stats(7, SEG)

            pe.wait_ge(S["h_ready"], 5 * KT)
            pe.wait_ge(S["consts"], 9)
            for t in range(2):
                for q in range(2):
                    for k in range(4 * q, 4 * q + 4):
                        ins = T.transpose(ps[2 * t + q][:, (k % 4) * P:(k % 4) * P + P], H3[:, k, t * P:t * P + P], ident[:, :])
                    ins.then_inc(S["h_tm"], 1)
            pe.wait_ge(S["rt_in"], 16)
            for t in range(2):
                for k in range(KT):
                    ins = T.matmul(ps[4][:, t * NE:t * NE + NE], H3[:, k, t * P:t * P + P], RT[:, k, :],
                                   start=(k == 0), stop=(k == KT - 1))
            ins.then_inc(S["logits"], 1)
            pe.wait_ge(S["sel"], 1)
            T.matmul(ps[5][:, 0:NE], BEFORE[:, :], SEL[:, 0, :], start=True, stop=True)
            T.matmul(ps[5][:, NE:2 * NE], ones[:, :], SEL[:, 0, :], start=True, stop=False)
            T.matmul(ps[5][:, NE:2 * NE], BEFORE[:, :], SEL[:, 1, :], start=False, stop=True)
            for t in range(2):
                ins = T.matmul(ps[5][:, 2 * NE:3 * NE], ones[:, :], SEL[:, t, :], start=(t == 0), stop=(t == 1))
            ins.then_inc(S["pos"], 1)
            pe.wait_ge(S["h_tm_out"], 4)
            pe.wait_ge(S["route"], 1)
            T.transpose(ps[7][:, 0:P], ident[:, :], ident[:, :]).then_inc(S["moe_w"], RING)

            def unit(n, u, k):
                v = cid_moe + u
                pe.wait_ge(w_in[v % RING], 16 * (v // RING + 1) + 16 * (UNITS // RING) * n)
                return slot(v, k)

            def item(n):
                pe.wait_ge(S["pg"], 4 * n + 4)
                for q in range(2):
                    pe.wait_ge(S["tr_out"], 7 * n)
                    for k in range(4 * q, 4 * q + 4):
                        for t in range(2):
                            ins = T.matmul(ps[4 + q][:, (k % 4) * P:(k % 4) * P + P], HTM[:, t, k * P:k * P + P],
                                           PG[:, t, :], start=(t == 0), stop=(t == 1))
                    ins.then_inc(S["xg"], 1)
                pe.wait_ge(S["yd_out"], 2 * n)
                for t in range(2):
                    ins = T.transpose(ps[6][:, t * P:t * P + P], PW[:, t, :], ident[:, :])
                ins.then_inc(S["xg"], 1)
                pe.wait_ge(S["xg_out"], 3 * n + 3)
                pe.wait_ge(S["sc_out"], 4 * n)
                u = 0

                def turn(j):
                    pe.wait_ge(S["hh"], 7 * n + j + 1)
                    if j >= 2:
                        pe.wait_ge(S["tr_out"], 7 * n + j - 1)
                    for q in range(4):
                        ins = T.transpose(ps[4 + j % 2][:, q * P:q * P + P], HH[:, j % 2, q * P:q * P + P], ident[:, :])
                    ins.then_inc(S["tr"], 1)
                for j in range(7):
                    if j >= 2:
                        pe.wait_ge(S["hh"], 7 * n + j - 1)
                    for half in range(2):
                        for kh in range(2):
                            w = unit(n, u, 4)
                            for k in range(4):
                                kk = 4 * kh + k
                                ins = T.matmul(ps[2 * (j % 2) + half][:, :], XG[:, kk, :], w[:, k, :],
                                               start=(kk == 0), stop=(kk == KT - 1))
                            ins.then_inc(S["moe_w"], 1)
                            u += 1
                    if j >= 1:
                        turn(j - 1)
                turn(6)
                for i in range(FE // SEG):
                    w = unit(n, u, 2)
                    if i % 2 == 0:
                        pe.wait_ge(S["tr_out"], 7 * n + i // 2 + 1)
                    for k in range(2):
                        for h in range(2):
                            ins = T.matmul(ps[6 + h][:, :], HX[:, 2 * i + k, :], w[:, k, 512 * h:512 * h + 512],
                                           start=(i == 0 and k == 0), stop=(i == FE // SEG - 1 and k == 1))
                    ins.then_inc(S["moe_w"], 1)
                    u += 1
                pe.wait_ge(S["yd_out"], 2 * n + 2)
                for k in range(KT):
                    ins = T.matmul(ps[k // 2][:, (k % 2) * SEG:(k % 2) * SEG + SEG], YS[:, k * P:k * P + P], PWT[:, :],
                                   start=True, stop=True)
                    if k % 2:
                        ins.then_inc(S["sc"], 1)
            with pe.Fori(0, NE) as e:
                item(e)
            items = second_items(pe, lambda e, n: item(n))
            pe.wait_ge(S["sc_out"], 4 * items)
            norm_stats(8, SEG)
            pe.wait_ge(S["post_done"], 4 * KT)
            for t in range(2):
                for q in range(2):
                    for k in range(4 * q, 4 * q + 4):
                        ins = T.transpose(ps[2 * t + q][:, (k % 4) * P:(k % 4) * P + P],
                                          X[:, k, SEG + t * P:SEG + t * P + P], ident[:, :])
                    ins.then_inc(S["out_t"], 1)

        @block.scalar
        def _(act):
            C = nc.scalar
            n_link = [0]

            def link(ins):
                n_link[0] += 1
                ins.then_inc(S["s_chain"], 1)
                act.wait_ge(S["s_chain"], n_link[0])

            def norm_stats(n, src, width):
                for k in range(KT):
                    if KT * n + k >= 2:
                        act.wait_ge(S["sq_used"], KT * n + k - 1)
                    C.activation(sq[:, (k % 2) * TOK:(k % 2) * TOK + width], src[:, k, :], ACT.Square).then_inc(S["sq_ready"], 1)
                act.wait_ge(S["sq_used"], KT * n + KT)
                C.activation(std[:, 0:width], ps[7][:, 0:width], ACT.Sqrt, scale=1.0 / D, bias=EPS).then_inc(S["std_ready"], 1)

            def modulate(m, dst, layer, sub, segs):
                for k in range(KT):
                    act.wait_ge(S["nt_ready"], KT * m + k + 1)
                    for q, sg in enumerate(segs):
                        ins = C.activation(dst[:, k, q * SEG:(q + 1) * SEG],
                                           ntmp[:, (k % 2) * TOK + q * SEG:(k % 2) * TOK + (q + 1) * SEG], ACT.Identity,
                                           scale=pre_gain(layer, sub, k, sg), bias=mod(layer, 3 * sub, k, sg))
                    ins.then_inc(S["h_ready"], 1)

            for k in range(KT):
                act.wait_ge(S["x_t"], k + 1)
                C.copy(X[:, k, :], ps[k % 6][:, :]).then_inc(S["x_t_out"], 1)
            act.wait_ge(S["vec_out"], 3)
            for n, name in enumerate(("c", "c_ctx")):
                C.activation(csil[:, n::2], vecs[:, VEC[name]:VEC[name] + KT], ACT.Silu).then_inc(S["csil"], 1)
            act.wait_ge(S["x_t_out"], KT)
            norm_stats(0, X, TOK)
            act.wait_ge(S["mod_out"], 1)
            modulate(0, H, 0, 0, (0, 1))

            tile = [0]

            def empty(dst, func=ACT.Copy, rows=P, width=TOK, **kw):
                n = tile[0]
                tile[0] += 1
                act.wait_ge(S["pj"], n + 1)
                src = ps[n % 6][0:rows, 0:width]
                if len(dst.shape) == 3:
                    src = src.rearrange("p (c t) -> p c t", c=SC)
                C.activation(dst, src, func, **kw).then_inc(S["pj_out"], 1)
            for h in range(GH):
                empty(K[:, h, :])
            for h in range(GH):
                empty(Q[:, h, :], scale=float(GDK) ** -0.5)
            empty(GL[0:32, :], rows=32)

            def prep(d, between):
                if d == 1:
                    act.wait_ge(S["gla_prep_v"], 5)
                    act.wait_ge(S["kd_t"], 4)
                for h in range(GH):
                    col = VEC["gla_b_g"] + GH * d + h
                    empty(LA[:, h, :], ACT.Identity, bias=vecs[:, col:col + 1])
                act.wait_ge(S["pj_out"], tile[0])
                between(0)
                link(C.activation(E[:, :, :], LA[:, :, :], ACT.Abs))
                link(C.activation(E[:, :, :], E[:, :, :], ACT.Exp, scale=-1.0))
                C.activation(E[:, :, :], E[:, :, :], ACT.Ln, bias=1.0).then_inc(S["gla_prep_s"], 1)
                between(1)
                act.wait_ge(S["gla_prep_v"], 5 * d + 1)
                C.activation(E[:, :, :], LA[:, :, :], ACT.Exp, scale=1.0 / 16).then_inc(S["gla_prep_s"], 1)
                between(2)
                act.wait_ge(S["gla_prep_v"], 5 * d + 2)
                C.activation(E[:, :, :], LA[:, :, :], ACT.Exp, scale=-1.0 / 16).then_inc(S["gla_prep_s"], 1)
                between(3)
                act.wait_ge(S["gla_prep_v"], 5 * d + 4)
                C.activation(E[:, :, :], LA[:, :, :], ACT.Exp, scale=-1.0 / 16).then_inc(S["gla_prep_s"], 1)

            def empty_v(i):
                for t in range(4):
                    empty(V[:, t, i * 256:(i + 1) * 256], width=256)

            def empty_r(i):
                for k in (2 * i, 2 * i + 1):
                    empty(R[:, k, :], ACT.Silu)

            prep(0, empty_v)
            prep(1, empty_r)

            for h in range(GH):
                act.wait_ge(S["sinter"], 2 * (NCH - 1) * (h + 1))
                for vt in range(2):
                    C.copy(Y1[:, 2 * h + vt, :], ps[2 + vt][:, :]).then_inc(S["y_out"], 1)
            act.wait_ge(S["y_out"], 2 * GH)
            for h in range(GH):
                for vt in range(2):
                    if h >= 1:
                        act.wait_ge(S["fn_ss"], 2 * h)
                    C.activation(sq[:, vt * TOK:vt * TOK + TOK], Y1[:, 2 * h + vt, :], ACT.Square).then_inc(S["fn_sq"], 1)
                act.wait_ge(S["fn_ss"], 2 * h + 2)
                if h >= 1:
                    act.wait_ge(S["fn_done"], 2 * h)
                C.activation(std[:, :], ps[h % 2][:, :], ACT.Sqrt, scale=1.0 / GDV, bias=EPS).then_inc(S["fn_std"], 1)
            for k in range(KT):
                empty(O1[:, k, :])
            act.wait_ge(S["pj_out"], tile[0])
            norm_stats(1, O1, TOK)
            act.wait_ge(S["post_done"], KT)
            norm_stats(2, X, TOK)
            modulate(1, H2, 0, 1, (0, 1))
            for p in range(FT // 2):
                for j in range(2):
                    n = 2 * p + j
                    if p >= 2:
                        act.wait_ge(S["ff_hid"], n - 3)
                    act.wait_ge(S["ff_mm"], 4 * p + j + 1)
                    C.activation(SIL[:, n % 4, :], ps[4 * (p % 2) + j][:, :], ACT.Silu).then_inc(S["ff_sil"], 1)
            act.wait_ge(S["ffd"], FT // 2)
            for k in range(KT):
                C.copy(O2[:, k, :], ps[k][:, :]).then_inc(S["ffd_out"], 1)
            act.wait_ge(S["ffd_out"], KT)
            norm_stats(3, O2, TOK)

            def pairs(v, p):
                return v[:, :, p, :]

            def norm_root(sg, p):
                act.wait_ge(S["kn_max"], HP * sg + p + 1)
                q = slice((p % 2) * TOK, (p % 2) * TOK + SEG)
                C.activation(ntmp[:, q], ntmp[:, q], ACT.Sqrt).then_inc(S["kn_sqrt"], 1)

            def segment(sg):
                act.wait_ge(S["post_done"], 2 * KT)
                norm_stats(4 + sg, X[:, :, tok_cols(sg)], SEG)
                modulate(2 + sg, HS, 1, 0, (sg,))
                for hid, func, base, dst in ((WL, ACT.Tanh, "rw_w0", SG), (AL, ACT.Copy, "rw_a0", AA)):
                    empty(hid[:, :], func, width=SEG)
                    for d in range(2):
                        for p in range(HP):
                            col = VEC[base] + HP * d + p
                            empty(pairs(dst[d], p), ACT.Sigmoid, width=SEG, bias=vecs[:, col:col + 1])
                for p in range(HP):
                    n = tile[0]
                    act.wait_ge(S["pj"], n + 1)
                    if p >= 2:
                        act.wait_ge(S["kn_mm"], HP * sg + p - 1)
                    col = VEC["rw_k_k"] + p
                    C.activation(sq[:, (p % 2) * TOK:(p % 2) * TOK + SEG], ps[n % 6][:, 0:SEG], ACT.Square,
                                 scale=vecs[:, col:col + 1]).then_inc(S["k_sq"], 1)
                    empty(pairs(KEY, p), width=SEG)
                    if p >= 2:
                        norm_root(sg, p - 2)
                norm_root(sg, HP - 2)
                norm_root(sg, HP - 1)
                for p in range(HP):
                    empty(pairs(VT, p), width=SEG)
                if sg:
                    for p in range(HP):
                        empty(pairs(RR, p), width=SEG)
                    empty(G1[:, :], ACT.Sigmoid, width=SEG)
                    empty(G2, ACT.Sigmoid, rows=GRK - P, width=SEG)
                act.wait_ge(S["pj_out"], tile[0])
                act.wait_ge(S["kn_done"], HP * (sg + 1))

            def before_scan(g):
                for d in range(2):
                    w = WORK[d]
                    act.wait_ge(pre_v[d], 3 * g + 2)
                    C.activation(w["e1"], w["e1"], ACT.Exp, scale=-DECAY).then_inc(pre_s[d], 1)
                    C.activation(w["e3"], w["sum"], ACT.Exp, scale=DECAY).then_inc(pre_s[d], 1)
                    act.wait_ge(pre_s[d], 3 * g + 2)
                    C.activation(w["e2"], w["sum"], ACT.Exp, scale=-DECAY).then_inc(pre_s[d], 1)

            def scan(lat, i):
                def step(d, dst, src, func, scale, need):
                    for c, n in need:
                        act.wait_ge(c.sems[d], c.value(lat, i, n))
                    C.activation(dst, src, func, scale=scale).then_inc(ac_s[d], 1)

                def bk(d, b):
                    return ps[4 * d + b][:, :].rearrange("p (a b) -> p a b", a=HP)
                w = WORK
                upper, lower = [(slice(r, r + CH), slice(None), slice(r, r + CH)) for r in (0, CH)]
                if i == 0:
                    act.wait_ge(S["off_zero"], 12 * (lat + 1))
                for d in range(2):
                    v = VT[:, i if d == 0 else SC - 1 - i]
                    step(d, w[d]["V"][upper], v[0:CH], ACT.Copy, 1.0, [])
                    step(d, w[d]["V"][lower], v[CH:P], ACT.Copy, 1.0, [])
                for d in range(2):
                    step(d, w[d]["NT"][upper], bk(d, 0)[0:CH], ACT.Copy, 1.0, [(PES, "NT")])
                    step(d, w[d]["NT"][lower], bk(d, 0)[CH:P], ACT.Copy, 1.0, [])
                for d in range(2):
                    act.wait_ge(pre_v[d], 3 * (SC * lat + i) + 3)
                    step(d, w[d]["A_bd"][upper], w[d]["A"][0:CH], ACT.Copy, 1.0, [])
                    step(d, w[d]["A_bd"][lower], w[d]["A"][CH:P], ACT.Copy, 1.0, [])
                for d in range(2):
                    v = two_banks(4 * d)
                    step(d, w[d]["Vt"][0:CH], v[upper], ACT.Copy, 1.0, [(PES, "Vt")])
                    step(d, w[d]["Vt"][CH:P], v[lower], ACT.Copy, 1.0, [])
                for d in range(2):
                    step(d, w[d]["B"], two_banks(4 * d + 2), ACT.Copy, 1.0, [(PES, "Bt")])
                for d in range(2):
                    step(d, w[d]["T"], two_banks(4 * d), ACT.Copy, 1.0, [(PES, "T0")])
                for d in range(2):
                    step(d, w[d]["K"], two_banks(4 * d + 2), ACT.Copy, 1.0, [(PES, "Kt")])
                for l in levels:
                    for d in range(2):
                        step(d, w[d]["X"], two_banks(4 * d), ACT.Copy, -1.0, [(PES, f"X{l}")])
                        if l > 1:
                            step(d, w[d]["TT"], two_banks(4 * d + 2), ACT.Copy, 1.0, [(PES, f"TT{l - 1}")])
                    if l == 3 and i < SC - 1:
                        before_scan(SC * lat + i + 1)
                for d in range(2):
                    step(d, w[d]["W"], bk(d, 0), ACT.Copy, -1.0, [(PES, "W")])
                for d in range(2):
                    step(d, w[d]["TT"], two_banks(4 * d + 2), ACT.Copy, 1.0, [(PES, "TT5")])
                for d in range(2):
                    step(d, w[d]["SA"], bk(d, 1), ACT.Copy, 1.0, [(PES, "SA")])

            for sg in range(2):
                segment(sg)
                before_scan(SC * sg)
                for i in range(SC):
                    scan(sg, i)
                for d in range(2):
                    act.wait_ge(dv_s[d], DVS.before(sg, SC))
            for p in range(HP):
                act.wait_ge(S["mean_sub"], p + 1)
                if p >= 2:
                    act.wait_ge(S["var_mm"], p - 1)
                C.activation(sq[:, (p % 2) * TOK:(p % 2) * TOK + SEG], pairs(YY, p), ACT.Square).then_inc(S["var_sq"], 1)
                act.wait_ge(S["var_mm"], p + 1)
                if p >= 1:
                    act.wait_ge(S["yn"], p)
                C.activation(std[:, 0:SEG], ps[4 + p % 2][:, 0:SEG], ACT.Sqrt, scale=1.0 / CH, bias=64e-5).then_inc(S["var_std"], 1)
            for k in range(KT):
                empty(O3[:, k, :], width=SEG)
            act.wait_ge(S["pj_out"], tile[0])
            norm_stats(6, O3, SEG)
            act.wait_ge(S["post_done"], 3 * KT)
            norm_stats(7, X[:, :, tok_cols(1)], SEG)
            modulate(4, H3, 1, 1, (1,))

            for n in range(4):
                act.wait_ge(S["h_tm"], n + 1)
                C.copy(HTM[:, n // 2, 512 * (n % 2):512 * (n % 2) + 512], ps[n][:, :]).then_inc(S["h_tm_out"], 1)
            act.wait_ge(S["ex_in"], 1)
            C.activation(EXL[:, :, :], EXL[:, :, :], ACT.Exp).then_inc(S["ex_out"], 1)

            def item(n):
                for q in range(2):
                    act.wait_ge(S["xg"], 3 * n + q + 1)
                    C.copy(XG[:, 4 * q:4 * q + 4, :], ps[4 + q][:, :].rearrange("p (a b) -> p a b", a=4)).then_inc(S["xg_out"], 1)
                act.wait_ge(S["xg"], 3 * n + 3)
                C.copy(PWT[:, :], ps[6][:, 0:SEG]).then_inc(S["xg_out"], 1)
                for j in range(8):
                    if j < 7:
                        act.wait_ge(S["moe_w"], RING + UNITS * n + 4 * j + 2)
                        if j >= 2:
                            act.wait_ge(S["hh"], 7 * n + j - 1)
                        C.activation(SX[:, j % 2, :], ps[2 * (j % 2)][:, :], ACT.Silu).then_inc(S["sil"], 1)
                    if j >= 1:
                        act.wait_ge(S["tr"], 7 * n + j)
                        C.copy(HX[:, 4 * (j - 1):4 * j, :], ps[4 + (j - 1) % 2][:, :].rearrange("p (a b) -> p a b", a=4))\
                            .then_inc(S["tr_out"], 1)
                act.wait_ge(S["moe_w"], RING + UNITS * (n + 1))
                for h in range(2):
                    C.copy(YS[:, 512 * h:512 * h + 512], ps[6 + h][:, :]).then_inc(S["yd_out"], 1)
            with act.Fori(0, NE) as e:
                item(e)
            items = second_items(act, lambda e, n: item(n))
            act.wait_ge(S["sc_out"], 4 * items)
            norm_stats(8, YA, SEG)
            for n in range(4):
                act.wait_ge(S["out_t"], n + 1)
                C.copy(OT[:, n // 2, 512 * (n % 2):512 * (n % 2) + 512], ps[n][:, :]).then_inc(S["out_c"], 1)

        @block.vector
        def _(dve):
            Vv = nc.vector
            n_link = [0]

            def link(ins):
                n_link[0] += 1
                ins.then_inc(S["v_chain"], 1)
                dve.wait_ge(S["v_chain"], n_link[0])

            def get_rstd(n, width, ready="std_ready"):
                dve.wait_ge(S[ready], n + 1)
                link(Vv.reciprocal(rstd[:, 0:width], std[:, 0:width]))

            def normalise(n, m, src, width):
                get_rstd(n, width)
                for k in range(KT):
                    if KT * m + k >= 2:
                        dve.wait_ge(S["h_ready"], KT * m + k - 1)
                    Vv.tensor_tensor(ntmp[:, (k % 2) * TOK:(k % 2) * TOK + width], src[:, k, :], rstd[:, 0:width],
                                     ALU.mult).then_inc(S["nt_ready"], 1)

            def post(n, src, width, layer, sub, segs):
                get_rstd(n, width)
                for k in range(KT):
                    link(Vv.tensor_tensor(src[:, k, :], src[:, k, :], rstd[:, 0:width], ALU.mult))
                    for q, sg in enumerate(segs):
                        cols = tok_cols(sg)
                        ins = Vv.scalar_tensor_tensor(X[:, k, cols], src[:, k, q * SEG:(q + 1) * SEG],
                                                      post_gain(layer, sub, k, sg), X[:, k, cols], ALU.mult, ALU.add)
                    ins.then_inc(S["post_done"], 1)
                    dve.wait_ge(S["post_done"], n_post[0] + k + 1)
                n_post[0] += KT
            n_post = [0]

            def add_bias(layer, lo, hi, bank):
                b = VEC["mod_b"] + 48 * layer
                return Vv.tensor_tensor(mods[:, 96 * layer + 2 * lo:96 * layer + 2 * hi].rearrange("p (j s) -> p j s", s=2),
                                        bank[:, 0:2 * (hi - lo)].rearrange("p (j s) -> p j s", s=2),
                                        vecs[:, b + lo:b + hi].unsqueeze(2).to_broadcast([P, hi - lo, 2]), ALU.add)

            def gains(layer):
                m = mods[:, 96 * layer:96 * layer + 96].rearrange("p (j s) -> p j s", s=2)
                for sub in range(2):
                    g = VEC["norm_g"] + 32 * layer + 16 * sub
                    o = (layer * 4 + 2 * sub) * 16
                    pre = gain[:, o:o + 16].rearrange("p (k s) -> p k s", s=2)
                    pst = gain[:, o + 16:o + 32].rearrange("p (k s) -> p k s", s=2)
                    link(Vv.scalar_tensor_tensor(pre, m[:, 24 * sub + 8:24 * sub + 16, :], 1.0,
                                                 vecs[:, g:g + 8].unsqueeze(2).to_broadcast([P, 8, 2]), ALU.add, ALU.mult))
                    ins = (Vv.tensor_tensor(pst, m[:, 24 * sub + 16:24 * sub + 24, :],
                                          vecs[:, g + 8:g + 16].unsqueeze(2).to_broadcast([P, 8, 2]), ALU.mult))
                    if sub == 0:
                        link(ins)
                ins.then_inc(S["mod_out"], 1)
                dve.wait_ge(S["mod_out"], layer + 1)

            for n in range(3):
                rows = sum(r for _, r in PACKS[n])
                dve.wait_ge(S["vec_t"], 3)
                Vv.tensor_copy(vecs[:, n * P:n * P + rows], ps[6][:, n * P:n * P + rows]).then_inc(S["vec_out"], 1)
            dve.wait_ge(S["vec_out"], 3)
            dve.wait_ge(S["mod_mm"], 24)
            link(add_bias(0, 0, 48, ps[6]))
            gains(0)
            dve.wait_ge(S["x_t_out"], KT)
            normalise(0, 0, X, TOK)

            for d in range(2):
                dve.wait_ge(S["gla_prep_s"], 4 * d + 1)
                link(Vv.tensor_scalar_min(LA[:, :, :], LA[:, :, :], 0.0))
                link(Vv.tensor_tensor(LA[:, :, :], LA[:, :, :], E[:, :, :], ALU.subtract))
                for h in range(GH):
                    row = LA[:, h, :] if d == 0 else LA[:, h, ::-1]
                    ins = Vv.tensor_tensor_scan(row, chunk_reset[:, :], row, 0.0, ALU.mult, ALU.add)
                ins.then_inc(S["gla_prep_v"], 1)
                dve.wait_ge(S["gla_prep_v"], 5 * d + 1)
                dve.wait_ge(S["gla_prep_s"], 4 * d + 2)
                if d == 0:
                    dve.wait_ge(S["pj_out"], 8)
                last = CH - 1 if d == 0 else 0
                Ec = E[:, :, :].rearrange("p h (c t) -> p h c t", t=CH)
                link(Vv.tensor_copy(DEC[d][:, :, :], Ec[:, :, :, last]))
                Vv.tensor_tensor(QD[d][:, :, :], Q[:, :, :], E[:, :, :], ALU.mult).then_inc(S["gla_prep_v"], 1)
                dve.wait_ge(S["gla_prep_s"], 4 * d + 3)
                if d == 0:
                    Vv.tensor_tensor(KI[d][:, :, :], K[:, :, :], E[:, :, :], ALU.mult).then_inc(S["gla_prep_v"], 1)
                else:
                    link(Vv.tensor_copy(KC[:, :, :], K[:, :, :]))
                    Vv.tensor_tensor(KI[d][:, :, :], K[:, :, :], E[:, :, :], ALU.mult).then_inc(S["gla_prep_v"], 1)
                for h in range(GH):
                    L = LA[:, h, :].rearrange("p (c t) -> p c t", t=CH)
                    link(Vv.tensor_copy(totals[:, 0:NCH], L[:, :, last]))
                    ins = Vv.tensor_tensor(L, L, totals[:, 0:NCH].unsqueeze(2).to_broadcast([P, NCH, CH]), ALU.subtract)
                    if h < GH - 1:
                        link(ins)
                ins.then_inc(S["gla_prep_v"], 1)
                dve.wait_ge(S["gla_prep_s"], 4 * d + 4)
                Vv.tensor_tensor(E[:, :, :], (K if d == 0 else KC)[:, :, :], E[:, :, :], ALU.mult).then_inc(S["gla_prep_v"], 1)
                for t in range(4):
                    n = 4 * d + t
                    dve.wait_ge(S["kd_t"], n + 1)
                    Vv.tensor_copy(KDT[d][:, t, :], ps[6 + n % 2][:, :]).then_inc(S["kd_t_out"], 1)
            for h in range(GH):
                dve.wait_ge(S["att"], 2 * h + 1)
                if h >= 2:
                    dve.wait_ge(S["sinter"], 2 * (NCH - 1) * (h - 1))
                m4 = [m[:, :].unsqueeze(1).to_broadcast([P, 4, P]) for m in (mask_fwd, mask_bwd)]
                Vv.tensor_tensor(ATT[:, h % 2, :].rearrange("p (a b) -> p a b", a=4),
                                 ps[0][:, :].rearrange("p (a b) -> p a b", a=4), m4[0], ALU.mult).then_inc(S["att_out"], 1)
                dve.wait_ge(S["att"], 2 * h + 2)
                Vv.tensor_tensor(ATB[:, :].rearrange("p (a b) -> p a b", a=4),
                                 ps[1][:, :].rearrange("p (a b) -> p a b", a=4), m4[1], ALU.mult).then_inc(S["att_out"], 1)
                dve.wait_ge(S["att_out"], 2 * h + 2)
                Vv.tensor_tensor(ATT[:, h % 2, :], ATT[:, h % 2, :], ATB[:, :], ALU.add).then_inc(S["att_m"], 1)
                for i in range(NCH - 1):
                    for d in range(2):
                        n = (NCH - 1) * h + i
                        c = i if d == 0 else (3 - i if i < 4 else 11 - i)
                        dve.wait_ge(S["sup"], 2 * n + d + 1)
                        if n >= 1:
                            dve.wait_ge(S["sinter"], 2 * (n - 1) + d + 1)
                        upd = ps[4 + d + 2 * (n % 2)][:, 0:GDV]
                        if i == 0:
                            ins = Vv.tensor_copy(ST[:, d, :], upd)
                        else:
                            dve.wait_ge(S["snew"], 2 * (n - 1) + d + 1)
                            ins = Vv.scalar_tensor_tensor(ST[:, d, :], ST[:, d, :], DEC[d][:, h, c:c + 1], upd,
                                                          ALU.mult, ALU.add)
                        ins.then_inc(S["snew"], 1)
            for h in range(GH):
                get_rstd(h, TOK, "fn_std")
                for vt in range(2):
                    k = 2 * h + vt
                    g = VEC["gla_norm_g"] + vt
                    link(Vv.tensor_tensor(Y1[:, k, :], Y1[:, k, :], rstd[:, :], ALU.mult))
                    Vv.scalar_tensor_tensor(Y1[:, k, :], Y1[:, k, :], vecs[:, g:g + 1], R[:, k, :],
                                            ALU.mult, ALU.mult).then_inc(S["fn_done"], 1)
            post(1, O1, TOK, 0, 0, (0, 1))
            normalise(2, 1, X, TOK)
            for n in range(FT):
                p, j = n // 2, n % 2
                if j == 0 and p >= 1:
                    lo, hi = mod_chunks[p - 1][0], mod_chunks[p - 1][-1] + 1
                    dve.wait_ge(S["mod_mm"], 24 + p)
                    add_bias(1, 2 * lo, 2 * hi, ps[4 * (p % 2) + 3]).then_inc(S["mod_part"], 1)
                if j == 0:
                    for i in range(len(mod_chunks[p])):
                        arrived(dve, first[f"mod1_{p}"] + i)
                        w = slot(first[f"mod1_{p}"] + i, KT)
                        for sg in range(2):
                            link(Vv.tensor_tensor(PROD[:, :, :], w, csil[:, sg::2].unsqueeze(2).to_broadcast([P, KT, SEG]), ALU.mult))
                            ins = Vv.reduce_sum(ACC[:, i, sg, :], PROD[:, :, :].rearrange("p k n -> p n k"), axis=AX.X)
                            if sg == 0:
                                link(ins)
                        ins.then_inc(S["mod_acc"], 1)
                        dve.wait_ge(S["mod_acc"], mod_chunks[p][i] + 1)
                dve.wait_ge(S["ff_sil"], n + 1)
                dve.wait_ge(S["ff_mm"], 4 * p + 2 + j + 1)
                Vv.tensor_tensor(HID[:, n, :], SIL[:, n % 4, :], ps[4 * (p % 2) + 2 + j][:, :], ALU.mult).then_inc(S["ff_hid"], 1)
            dve.wait_ge(S["mod_part"], n_pairs - 1)
            gains(1)
            post(3, O2, TOK, 0, 1, (0, 1))

            jn = [0]

            def minus(out_, a, b):
                link(Vv.tensor_tensor(out_, a, b, ALU.subtract))

            def negated(out_, a):
                link(Vv.tensor_scalar(out_, a, -1.0, None, ALU.mult))

            def shift(sg):
                if sg == 0:
                    lo, hi = slice(0, KT // 2), slice(KT // 2, KT)
                    minus(XX[:, lo, 1:SEG], HS[:, lo, 0:SEG - 1], HS[:, lo, 1:SEG])
                    negated(XX[:, lo, 0:1], HS[:, lo, 0:1])
                    minus(XX[:, hi, 0:SEG - 1], HS[:, hi, 1:SEG], HS[:, hi, 0:SEG - 1])
                    negated(XX[:, hi, SEG - 1:SEG], HS[:, hi, SEG - 1:SEG])
                    return
                for k in range(4):
                    g, h = (v[:, k, :].rearrange("p (r c) -> p r c", c=GW) for v in (XX, HS))
                    if k < 2:
                        minus(g[:, :, 1:GW], h[:, :, 0:GW - 1], h[:, :, 1:GW])
                        negated(g[:, :, 0:1], h[:, :, 0:1])
                    else:
                        minus(g[:, :, 0:GW - 1], h[:, :, 1:GW], h[:, :, 0:GW - 1])
                        negated(g[:, :, GW - 1:GW], h[:, :, GW - 1:GW])
                minus(XX[:, 4:6, GW:SEG], HS[:, 4:6, 0:SEG - GW], HS[:, 4:6, GW:SEG])
                negated(XX[:, 4:6, 0:GW], HS[:, 4:6, 0:GW])
                minus(XX[:, 6:8, 0:SEG - GW], HS[:, 6:8, GW:SEG], HS[:, 6:8, 0:SEG - GW])
                negated(XX[:, 6:8, SEG - GW:SEG], HS[:, 6:8, SEG - GW:SEG])

            def segment(sg):
                normalise(4 + sg, 2 + sg, X[:, :, tok_cols(sg)], SEG)
                dve.wait_ge(S["h_ready"], KT * (3 + sg))
                shift(sg)
                for j in (1, 4, 2, 3, 0, 5)[:4 + 2 * sg]:
                    n = jn[0]
                    jn[0] += 1
                    if n >= 2:
                        dve.wait_ge(S["pj"], MIX_DONE[n - 2])
                    for k in range(KT):
                        col = VEC["rw_mu"] + KT * j + k
                        ins = Vv.scalar_tensor_tensor(XJ[n % 2][:, k, :], XX[:, k, :], vecs[:, col:col + 1], HS[:, k, :],
                                                      ALU.mult, ALU.add)
                    ins.then_inc(S["mix_ready"], 1)
                    if j == 3:
                        keys(sg)

            def keys(sg):
                if sg == 0:
                    link(Vv.tensor_scalar(KAM[:, :], vecs[:, VEC["rw_k_a"]:VEC["rw_k_a"] + HP], -1.0, 1.0, ALU.mult, ALU.add))
                for p in range(HP + 1):
                    if p < HP:
                        q = slice((p % 2) * TOK, (p % 2) * TOK + SEG)
                        dve.wait_ge(S["kn_mm"], HP * sg + p + 1)
                        if p >= 2:
                            dve.wait_ge(S["kn_rcp"], HP * sg + p - 1)
                        Vv.tensor_scalar(ntmp[:, q], ps[6 + p % 2][:, 0:SEG], 1e-24, None, ALU.max).then_inc(S["kn_max"], 1)
                    if p >= 1:
                        o = p - 1
                        q = slice((o % 2) * TOK, (o % 2) * TOK + SEG)
                        dve.wait_ge(S["kn_sqrt"], HP * sg + o + 1)
                        dve.wait_ge(S["kn_done"], HP * sg + o)
                        Vv.reciprocal(rstd[:, 0:SEG], ntmp[:, q]).then_inc(S["kn_rcp"], 1)
                        dve.wait_ge(S["kn_rcp"], HP * sg + o + 1)
                        dve.wait_ge(S["pj_out"], KEY_PJ[sg] + o + 1)
                        col = VEC["rw_k_k"] + o
                        Vv.scalar_tensor_tensor(KK[:, :, o, :], KEY[:, :, o, :], vecs[:, col:col + 1],
                                                rstd[:, 0:SEG].rearrange("p (c t) -> p c t", c=SC),
                                                ALU.mult, ALU.mult).then_inc(S["kn_done"], 1)

            def pick(v, d, g):
                return v[:, g % SC if d == 0 else SC - 1 - g % SC, :, :]

            def sums(g):
                for d in range(2):
                    w = WORK[d]
                    sg_c = pick(SG[d], d, g).rearrange("p a b -> p (a b)")
                    run = w["sum"].rearrange("p a b -> p (a b)")
                    if d == 1:
                        sg_c, run = sg_c[:, ::-1], run[:, ::-1]
                    Vv.tensor_tensor_scan(run, chunk_reset[:, :], sg_c, 0.0, ALU.mult, ALU.add).then_inc(pre_v[d], 1)
                for d in range(2):
                    w = WORK[d]
                    dve.wait_ge(pre_v[d], 3 * g + 1)
                    Vv.tensor_tensor(w["e1"], w["sum"], pick(SG[d], d, g), ALU.subtract).then_inc(pre_v[d], 1)

            def removal(g):
                for d in range(2):
                    dve.wait_ge(pre_s[d], 3 * g + 1)
                    Vv.tensor_tensor(WORK[d]["A"], pick(KK, d, g), WORK[d]["e1"], ALU.mult).then_inc(pre_v[d], 1)

            def scan(lat, i):
                w = WORK

                def bk(d, b):
                    return ps[4 * d + b][:, :].rearrange("p (a b) -> p a b", a=HP)

                def over(v):
                    return v.unsqueeze(1).to_broadcast([P, HP, CH])

                def vec(v):
                    return v.unsqueeze(2).to_broadcast([P, HP, CH])

                def need(d, *what):
                    for c, n in what:
                        dve.wait_ge(c.sems[d], c.value(lat, i, n))
                    dve.wait_ge(dv_s[d], DVS.before(lat, i) + said[d])

                def said_one(d):
                    said[d] += 1
                said = [0, 0]

                def mult(d, dst, a, b, *what):
                    need(d, *what)
                    Vv.tensor_tensor(dst, a, b, ALU.mult).then_inc(dv_s[d], 1)
                    said_one(d)

                def add(d, dst, a, b, *what):
                    need(d, *what)
                    Vv.tensor_tensor(dst, a, b, ALU.add).then_inc(dv_s[d], 1)
                    said_one(d)

                def by_blocks(d, dst, a, b):
                    for r in (slice(0, CH), slice(CH, P)):
                        mult(d, dst[r, :, r], a[r], b[r])
                ka = vecs[:, VEC["rw_k_a"]:VEC["rw_k_a"] + HP]
                for d in range(2):
                    dve.wait_ge(pe_s[d], PES.before(lat, i))
                for d in range(2):
                    if i == 0 and d == 0:
                        dve.wait_ge(S["off_zero"], 12 * (lat + 1))
                    dve.wait_ge(pre_v[d], 3 * (SC * lat + i) + 3)
                    mult(d, w[d]["kka"], pick(KK, d, i), pick(AA[d], d, i))
                    dve.wait_ge(pre_s[d], 3 * (SC * lat + i) + 3)
                    by_blocks(d, w[d]["B"], w[d]["kka"], w[d]["e3"])
                    if lat:
                        mult(d, w[d]["R"], pick(RR, d, i), w[d]["e2"])
                    need(d)
                    Vv.tensor_copy(PC[d], w[d]["e2"][:, :, CH - 1 if d == 0 else 0]).then_inc(dv_s[d], 1)
                    said_one(d)
                for d in range(2):
                    mult(d, w[d]["t"], pick(AA[d], d, i), vec(ka))
                    add(d, w[d]["t"], w[d]["t"], vec(KAM))
                    mult(d, w[d]["t"], w[d]["t"], pick(KEY, d, i))
                    by_blocks(d, w[d]["K"], w[d]["t"], w[d]["e3"])

                def blocks(v):
                    return v.rearrange("p a (q b) -> p (a q) b", q=2)

                def over2(v, n=2 * HP):
                    return v.unsqueeze(1).to_broadcast([P, n, v.shape[-1]])
                for d in range(2):
                    mult(d, blocks(w[d]["TT"]), blocks(w[d]["NT"]), over2(LM[0][d]), (ACS, "NT"))
                    need(d)
                    Vv.tensor_tensor(w[d]["TT"], over2(ident[:, :], HP), w[d]["TT"], ALU.subtract).then_inc(dv_s[d], 1)
                    said_one(d)
                    mult(d, blocks(w[d]["NTl"]), blocks(w[d]["NT"]), over2(LM[1][d]))
                    if lat:
                        mult(d, w[d]["Mrb"], bk(d, 1), over(INCL[d]), (PES, "Mrb"))
                    need(d, (PES, "Lak"))
                    by_blocks(d, w[d]["Lak"], bk(d, 2), over(STRICT[d]))
                if lat:
                    for d in range(2):
                        mult(d, w[d]["Mrk"], bk(d, 3), over(INCL[d]), (PES, "Mrk"))
                for l in levels:
                    if l < 5:
                        for d in range(2):
                            mult(d, blocks(w[d]["NTl"]), blocks(w[d]["NT"]), over2(LM[l + 1][d]), (PES, f"X{l}"))
                    for d in range(2):
                        add(d, w[d]["T"], w[d]["T"], two_banks(4 * d + 2), (PES, f"TX{l}"))
                    if l == 2 and i < SC - 1:
                        for d in range(2):
                            need(d, (ACS, "A_bd"))
                        sums(SC * lat + i + 1)
                    if l == 3 and i < SC - 1:
                        removal(SC * lat + i + 1)
                for d in range(2):
                    if lat:
                        add(d, pick(YY, d, i), pick(YY, d, i), bk(d, 3), (PES, "y"))
                    add(d, w[d]["ST"], w[d]["ST"], bk(d, 2), (PES, "U"))
                    mult(d, w[d]["ST"], w[d]["ST"], vec(PC[d]), (DVS, "U"))

            for sg in range(2):
                segment(sg)
                dve.wait_ge(S["mix_ready"], 4 + 6 * sg)
                if sg == 0:
                    for d in range(2):
                        Vv.memset(WORK[d]["ST"], 0.0).then_inc(S["st_zero"], 1)
                    dve.wait_ge(S["st_zero"], 2)
                else:
                    link(Vv.memset(YY[:, :, :, :], 0.0))
                dve.wait_ge(S["pj_out"], PROJ_END[sg])
                dve.wait_ge(S["kn_done"], HP * (sg + 1))
                sums(SC * sg)
                removal(SC * sg)
                for i in range(SC):
                    scan(sg, i)
            for d in range(2):
                dve.wait_ge(dv_s[d], DVS.before(1, SC))
            link(Vv.scalar_tensor_tensor(U1[:, :, :, :].rearrange("p c a b -> p (c a b)"),
                                         AA[0][:, :, :, :].rearrange("p c a b -> p (c a b)"), -2.0,
                                         AA[1][:, :, :, :].rearrange("p c a b -> p (c a b)"), ALU.add, ALU.add))
            for p in range(HP):
                u, k = U1[:, :, p, :], VEC["rw_k_a"] + p
                link(Vv.tensor_scalar(u, u, vecs[:, k:k + 1], 2.0, ALU.mult, ALU.add))
                link(Vv.tensor_tensor(u, u, KEY[:, :, p, :], ALU.mult))
                k = VEC["rw_r_k"] + p
                Vv.scalar_tensor_tensor(u, u, vecs[:, k:k + 1], RR[:, :, p, :], ALU.mult, ALU.mult).then_inc(S["u_ready"], 1)

            def bank3(b):
                return ps[b][:, 0:SEG].rearrange("p (c t) -> p c t", c=SC)
            for p in range(HP):
                dve.wait_ge(S["b_mm"], p + 1)
                Vv.tensor_tensor(VT[:, :, p, :], VT[:, :, p, :], bank3(p % 2), ALU.mult).then_inc(S["b_out"], 1)
            for p in range(HP):
                dve.wait_ge(S["mean_mm"], p + 1)
                Vv.scalar_tensor_tensor(YY[:, :, p, :], bank3(2 + p % 2), -1.0 / CH, YY[:, :, p, :],
                                        ALU.mult, ALU.add).then_inc(S["mean_sub"], 1)
            for p in range(HP):
                y = YY[:, :, p, :]
                dve.wait_ge(S["var_std"], p + 1)
                link(Vv.reciprocal(rstd[:, 0:SEG], std[:, 0:SEG]))
                Vv.tensor_tensor(y, y, rstd[:, 0:SEG].rearrange("p (c t) -> p c t", c=SC), ALU.mult).then_inc(S["yn"], 1)
                dve.wait_ge(S["yn"], p + 1)
                gc, bc = VEC["rw_ln_g"] + p, VEC["rw_ln_b"] + p
                link(Vv.tensor_scalar(y, y, vecs[:, gc:gc + 1], vecs[:, bc:bc + 1], ALU.mult, ALU.add))
                dve.wait_ge(S["b_out"], p + 1)
                link(Vv.tensor_tensor(y, y, VT[:, :, p, :], ALU.add))
                dve.wait_ge(S["gate_mm"], p + 1)
                Vv.tensor_tensor(y, y, bank3(6 + p % 2), ALU.mult).then_inc(S["o_in"], 1)
            post(6, O3, SEG, 1, 0, (1,))
            normalise(7, 4, X[:, :, tok_cols(1)], SEG)

            dve.wait_ge(S["logits"], 1)
            dve.wait_ge(S["consts"], 9)
            link(Vv.tensor_copy(LOG[:, :, :], ps[4][:, 0:2 * NE].rearrange("p (a b) -> p a b", a=2)))
            for t in range(2):
                mine = LOG[:, t, :].unsqueeze(2).to_broadcast([P, NE, NE])
                other = LOG[:, t, :].unsqueeze(1).to_broadcast([P, NE, NE])
                link(Vv.tensor_tensor(GT[:, t, :, :], other, mine, ALU.is_gt))
                link(Vv.tensor_tensor(EQ[:, t, :, :], other, mine, ALU.is_equal))
                link(Vv.tensor_tensor(EQ[:, t, :, :], EQ[:, t, :, :], TRI[:, :, :], ALU.mult))
                link(Vv.tensor_tensor(GT[:, t, :, :], GT[:, t, :, :], EQ[:, t, :, :], ALU.add))
                link(Vv.reduce_sum(SEL[:, t, :], GT[:, t, :, :], axis=AX.X))
                link(Vv.reduce_max(MX[:, t:t + 1], LOG[:, t, :], axis=AX.X))
            for t in range(2):
                ins = Vv.tensor_scalar(EXL[:, t, :], LOG[:, t, :], MX[:, t:t + 1], None, ALU.subtract)
            ins.then_inc(S["ex_in"], 1)
            Vv.tensor_scalar(SEL[:, :, :], SEL[:, :, :], 1.5, None, ALU.is_lt).then_inc(S["sel"], 1)
            dve.wait_ge(S["sel"], 1)
            dve.wait_ge(S["ex_out"], 1)
            link(Vv.tensor_tensor(CMB[:, :, :], SEL[:, :, :], EXL[:, :, :], ALU.mult))
            link(Vv.reduce_sum(MX[:, :], CMB[:, :, :], axis=AX.X))
            link(Vv.reciprocal(MX[:, :], MX[:, :]))
            link(Vv.tensor_tensor(CMB[:, :, :], CMB[:, :, :], MX[:, :].unsqueeze(2).to_broadcast([P, 2, NE]), ALU.mult))
            dve.wait_ge(S["pos"], 1)
            link(Vv.scalar_tensor_tensor(RK0[:, :, :], ps[5][:, 0:2 * NE].rearrange("p (a b) -> p a b", a=2), 1.0,
                                         SEL[:, :, :], ALU.add, ALU.mult))
            link(Vv.tensor_scalar(RK0[:, :, :], RK0[:, :, :], -1.0, None, ALU.add))
            link(Vv.tensor_scalar(RK1[:, :, :], RK0[:, :, :], -float(P), None, ALU.add))
            over, last, tmp = MORE[:, 0:NE], MORE[:, NE:2 * NE], MORE[:, 2 * NE:3 * NE]
            link(Vv.memset(tmp, 1.0))
            link(Vv.tensor_scalar(over, ps[5][:, 2 * NE:3 * NE], P + 0.5, None, ALU.is_gt))
            link(Vv.tensor_tensor_scan(last, tmp, over, float(NE), ALU.mult, ALU.add))
            link(Vv.tensor_copy(more_i[:, 2 * NE:2 * NE + 1], last[:, NE - 1:NE]))
            link(Vv.tensor_tensor(tmp, last, over, ALU.subtract))
            link(Vv.tensor_copy(more_i[:, 0:NE], over))
            Vv.tensor_copy(more_i[:, NE:2 * NE], tmp).then_inc(S["route"], 1)
            dve.wait_ge(S["route"], 1)

            def item(part, e, n):
                rk = (RK0, RK1)[part]
                dve.wait_ge(S["sc_out"], 4 * n)
                dve.wait_ge(S["xg"], 3 * n)
                for t in range(2):
                    pos = rk[:, t, :][:, bass.ds(e, 1)]
                    wt = CMB[:, t, :][:, bass.ds(e, 1)]
                    Vv.tensor_scalar(PG[:, t, :], SLOTS[:, :], pos, None, ALU.is_equal).then_inc(S["pg"], 1)
                    Vv.tensor_scalar(PW[:, t, :], SLOTS[:, :], pos, wt, ALU.is_equal, ALU.mult).then_inc(S["pg"], 1)
                for j in range(7):
                    dve.wait_ge(S["sil"], 7 * n + j + 1)
                    dve.wait_ge(S["moe_w"], RING + UNITS * n + 4 * j + 4)
                    if j >= 2:
                        dve.wait_ge(S["tr"], 7 * n + j - 1)
                    Vv.tensor_tensor(HH[:, j % 2, :], SX[:, j % 2, :], ps[2 * (j % 2) + 1][:, :], ALU.mult).then_inc(S["hh"], 1)
                for q in range(4):
                    dve.wait_ge(S["sc"], 4 * n + q + 1)
                    v = YA[:, 2 * q:2 * q + 2, :]
                    Vv.tensor_tensor(v, v, ps[q][:, :].rearrange("p (a b) -> p a b", a=2), ALU.add).then_inc(S["sc_out"], 1)
            with dve.Fori(0, NE) as e:
                item(0, e, e)
            second_items(dve, lambda e, n: item(1, e, n))
            post(8, YA, SEG, 1, 1, (1,))

_INS = ["x", "c", "ctx", "c_ctx", "mod_w", "mod_b", "norm_g", "gla_w_in", "gla_w_g2", "gla_b_g", "gla_norm_g",
        "gla_w_out", "rw_mu", "rw_w_rkv", "rw_w_o", "rw_w0", "rw_w1", "rw_w2", "rw_a0", "rw_a1", "rw_a2", "rw_g1",
        "rw_g2", "rw_k_k", "rw_k_a", "rw_r_k", "rw_ln_g", "rw_ln_b", "ff_w_gu", "ff_w_d", "moe_router", "moe_w_gu",
        "moe_w_d"]

def kernel(**inputs):
    import concourse.bacc as bacc
    from concourse.bass_utils import run_bass_kernel_spmd

    nc = bacc.Bacc("TRN2", target_bir_lowering=False, num_devices=1)
    arrays, aps = {}, {}
    for name in _INS:
        a = np.ascontiguousarray(inputs[name])
        arrays["in_" + name] = a
        aps[name] = nc.dram_tensor("in_" + name, a.shape, mybir.dt.from_np(a.dtype), kind="ExternalInput").ap()
    out = nc.dram_tensor("out", (1, SEG, D), F32, kind="ExternalOutput").ap()
    hybrid_backbone(nc, aps, out)
    return run_bass_kernel_spmd(nc, [arrays], core_ids=[0]).results[0]["out"]
```
